# Optimizing a Trainium2 kernel written in Bass

```python
import jax
import jax.numpy as jnp
from jax import lax
import numpy as np

D_MODEL = 1024
BATCH = 1
SEQ = 128
DEPTH = 2
DEC_BATCH = 1
DEC_SEQ = 512
PAST_LEN = 128

GRID_W = 64
EPS = 1e-6
N_MOD = 6
SSD_HEADDIM = 64
SSD_HEADS = D_MODEL // SSD_HEADDIM
SSD_INNER = SSD_HEADS * SSD_HEADDIM
SSD_GROUPS = 2
SSD_STATE = 128
SSD_CONV_W = 3
SSD_CHUNK = 128
SSD_XBC = SSD_INNER + 2 * SSD_GROUPS * SSD_STATE
SC_WIDTH = D_MODEL
SC_CONV_W = 3
MIX0_IN = SSD_INNER + SSD_XBC + 2 * SSD_HEADS + 3 * SC_WIDTH
MIX0_OUT = SSD_INNER + SC_WIDTH
NA_HEAD_DIM = 64
NA_HEADS = D_MODEL // NA_HEAD_DIM
NA_INNER = NA_HEADS * NA_HEAD_DIM
NA_KH = 8
NA_KW = 16
Q_BLOCK = 128
D_FF = ((8 * D_MODEL // 3 + 255) // 256) * 256
FFN_CONV_W = 3
N_SSD_LAYERS = (DEPTH + 1) // 2
N_NA_LAYERS = DEPTH // 2

kernel_name = 'hybrid_ssd_conv_natten_prefix_dit_step'

def rmsnorm(x, g):
    xf = x.astype(jnp.float32)
    y = xf * lax.rsqrt(jnp.mean(xf * xf, axis=-1, keepdims=True) + EPS)
    return (y * g.astype(jnp.float32)).astype(x.dtype)

def dwconv(x, w):
    k, ch = w.shape
    pl = (k - 1) // 2
    return lax.conv_general_dilated(x, w[:, None, :].astype(x.dtype), window_strides=(1,),
                                    padding=[(pl, k - 1 - pl)], dimension_numbers=('NWC', 'WIO', 'NWC'),
                                    feature_group_count=ch)

def ssd_scan(x, dt, a, bm, cm, h0):
    b, l, h, p = x.shape
    nc = l // SSD_CHUNK

    def chunks(t):
        return t.reshape((b, nc, SSD_CHUNK) + t.shape[2:])

    xd = chunks(x * dt[..., None])
    bm, cm = chunks(bm), chunks(cm)
    a_cs = jnp.cumsum(jnp.moveaxis(chunks(dt * a), -1, 1), axis=-1)
    causal = jnp.tril(jnp.ones((SSD_CHUNK, SSD_CHUNK), dtype=bool))
    seg = a_cs[..., :, None] - a_cs[..., None, :]
    decay = jnp.where(causal, jnp.exp(jnp.where(causal, seg, 0.0)), 0.0)
    cb = jnp.einsum('bclhn,bcshn->bhcls', cm, bm) * decay
    y = jnp.einsum('bhcls,bcshp->bclhp', cb, xd)
    to_end = jnp.exp(a_cs[..., -1:] - a_cs)
    st = jnp.einsum('bclhn,bhcl,bclhp->bchpn', bm, to_end, xd)
    chunk_decay = jnp.exp(a_cs[..., -1])

    def step(hc, inp):
        s_c, d_c = inp
        return hc * d_c[..., None, None] + s_c, hc

    h_final, h_in = lax.scan(step, h0, (jnp.moveaxis(st, 1, 0), jnp.moveaxis(chunk_decay, -1, 0)))
    y = y + jnp.einsum('bclhn,cbhpn,bhcl->bclhp', cm, h_in, jnp.exp(a_cs))
    return y.reshape(b, l, h, p), h_final

def ssd_mixer(z, xbc, dt_raw, conv_w, conv_b, dt_bias, a_log, d_skip, norm_g, h0):
    b, l, _ = z.shape
    xbc = jax.nn.silu(dwconv(xbc, conv_w) + conv_b).astype(jnp.float32)
    xs, bm, cm = jnp.split(xbc, [SSD_INNER, SSD_INNER + SSD_GROUPS * SSD_STATE], axis=-1)
    xs = xs.reshape(b, l, SSD_HEADS, SSD_HEADDIM)
    rep = SSD_HEADS // SSD_GROUPS
    bm = jnp.repeat(bm.reshape(b, l, SSD_GROUPS, SSD_STATE), rep, axis=2)
    cm = jnp.repeat(cm.reshape(b, l, SSD_GROUPS, SSD_STATE), rep, axis=2)
    dt = jax.nn.softplus(dt_raw.astype(jnp.float32).reshape(b, l, 2, SSD_HEADS) + dt_bias.astype(jnp.float32))
    a = -jnp.exp(a_log.astype(jnp.float32))
    h0 = h0.astype(jnp.float32)
    y_f, s_f = ssd_scan(xs, dt[:, :, 0], a[0], bm, cm, h0[:, 0])

    def flip(t):
        return jnp.flip(t, axis=1)

    y_b, s_b = ssd_scan(flip(xs), flip(dt[:, :, 1]), a[1], flip(bm), flip(cm), h0[:, 1])
    y = y_f + flip(y_b) + xs * jnp.sum(d_skip.astype(jnp.float32), axis=0)[:, None]
    y = y.reshape(b, l, SSD_INNER) * jax.nn.silu(z.astype(jnp.float32))
    y = rmsnorm(y, norm_g).astype(z.dtype)
    return y, jnp.stack([s_f, s_b], axis=1)

def mixer_ssd_conv(h, P, e, h0):
    u = h @ P['ssd_w_in'][e]
    s1 = SSD_INNER
    s2 = s1 + SSD_XBC
    s3 = s2 + 2 * SSD_HEADS
    s4 = s3 + SC_WIDTH
    s5 = s4 + SC_WIDTH
    z, xbc, dt_raw, bg, cg, xin = jnp.split(u, [s1, s2, s3, s4, s5], axis=-1)
    y_a, states = ssd_mixer(z, xbc, dt_raw, P['ssd_conv_w'][e], P['ssd_conv_b'][e], P['ssd_dt_bias'][e],
                            P['ssd_a_log'][e], P['ssd_d'][e], P['ssd_norm_g'][e], h0)
    y_b = bg * dwconv(cg * xin, P['sc_conv_w'][e])
    return jnp.concatenate([y_a, y_b], axis=-1) @ P['mix0_w_out'][e], states

def split_heads(t, b, l):
    return t.reshape(b, l, NA_HEADS, NA_HEAD_DIM)

def dense_context_attention(q, k, v):
    b, s, h, d = q.shape
    qb = jnp.moveaxis(q.reshape(b, s // Q_BLOCK, Q_BLOCK, h, d), 1, 0)

    def one_block(qi):
        sc = jnp.einsum('bqhd,bkhd->bhqk', qi, k).astype(jnp.float32) * (d ** -0.5)
        p = jax.nn.softmax(sc, axis=-1).astype(v.dtype)
        return jnp.einsum('bhqk,bkhd->bqhd', p, v)

    o = lax.map(one_block, qb)
    return jnp.moveaxis(o, 0, 1).reshape(b, s, h * d)

def na_context(h, P, o):
    b, s, _ = h.shape
    q, k, v = [split_heads(t, b, s) for t in jnp.split(h @ P['na_w_qkv'][o], 3, axis=-1)]
    y = dense_context_attention(q, k, v)
    return y @ P['na_w_out'][o], k, v

def na_latent(h, P, o, k_ctx, v_ctx):
    b, l, _ = h.shape
    rows = l // GRID_W
    kh = min(NA_KH, rows)
    nb = GRID_W // NA_KW
    span = 2 * NA_KW
    q, k, v = [split_heads(t, b, l) for t in jnp.split(h @ P['na_w_qkv'][o], 3, axis=-1)]
    r = np.arange(rows)
    row_idx = np.clip(r - kh // 2, 0, rows - kh)[:, None] + np.arange(kh)
    qcol = np.arange(GRID_W).reshape(nb, NA_KW)
    col_idx = np.clip(np.arange(nb) * NA_KW - NA_KW // 2, 0, GRID_W - span)[:, None] + np.arange(span)
    col_start = np.clip(qcol - NA_KW // 2, 0, GRID_W - NA_KW)
    col_ok = (col_idx[:, None, :] >= col_start[:, :, None]) & (col_idx[:, None, :] < col_start[:, :, None] + NA_KW)
    dr = row_idx - r[:, None] + NA_KH - 1
    dc = np.clip(col_idx[:, None, :] - qcol[:, :, None] + NA_KW - 1, 0, 2 * NA_KW - 2)
    rpb = P['na_rpb'][o].astype(jnp.float32)
    bias = rpb[:, dr[:, None, None, :, None], dc[None, :, :, None, :]]
    bias = jnp.where(col_ok[None, None, :, :, None, :], bias, -jnp.inf)
    bias = jnp.moveaxis(bias, 0, 2).reshape(rows, nb, NA_HEADS, NA_KW, kh * span)
    kg = k.reshape(b, rows, GRID_W, NA_HEADS, NA_HEAD_DIM)
    vg = v.reshape(b, rows, GRID_W, NA_HEADS, NA_HEAD_DIM)
    ri = row_idx[:, None, :, None]
    ci = col_idx[None, :, None, :]
    n_loc = kh * span
    k_loc = kg[:, ri, ci].reshape(b, rows, nb, n_loc, NA_HEADS, NA_HEAD_DIM)
    v_loc = vg[:, ri, ci].reshape(b, rows, nb, n_loc, NA_HEADS, NA_HEAD_DIM)
    qb = q.reshape(b, rows, nb, NA_KW, NA_HEADS, NA_HEAD_DIM)
    scale = NA_HEAD_DIM ** -0.5
    s_loc = jnp.einsum('brjqhd,brjkhd->brjhqk', qb, k_loc).astype(jnp.float32) * scale + bias
    s_ctx = jnp.einsum('brjqhd,bshd->brjhqs', qb, k_ctx).astype(jnp.float32) * scale
    p = jax.nn.softmax(jnp.concatenate([s_loc, s_ctx], axis=-1), axis=-1).astype(v.dtype)
    out = (jnp.einsum('brjhqk,brjkhd->brjqhd', p[..., :n_loc], v_loc)
           + jnp.einsum('brjhqs,bshd->brjqhd', p[..., n_loc:], v_ctx))
    return out.reshape(b, l, NA_INNER) @ P['na_w_out'][o]

def conv_ffn(h, P, i):
    g = dwconv(h @ P['ffn_w_gate'][i], P['ffn_conv_w'][i])
    u = h @ P['ffn_w_up'][i]
    return (jax.nn.gelu(g) * u) @ P['ffn_w_down'][i]

def run_stream(x, cvec, P, is_ctx, state_ssd, cache_k, cache_v):
    new_ssd, new_k, new_v = [], [], []
    b = x.shape[0]
    for i in range(DEPTH):
        m = jax.nn.silu(cvec) @ P['ada_w'][i] + P['ada_b'][i]
        sh1, sc1, g1, sh2, sc2, g2 = jnp.split(m[:, None, :].astype(x.dtype), N_MOD, axis=-1)
        h = rmsnorm(x, P['norm_mix_g'][i]) * (1 + sc1) + sh1
        if i % 2 == 0:
            e = i // 2
            if is_ctx:
                h0 = jnp.zeros((b, 2, SSD_HEADS, SSD_HEADDIM, SSD_STATE), jnp.float32)
            else:
                h0 = state_ssd[:, e]
            y, st = mixer_ssd_conv(h, P, e, h0)
            new_ssd.append(st.astype(x.dtype))
        else:
            o = i // 2
            if is_ctx:
                y, k, v = na_context(h, P, o)
                new_k.append(k)
                new_v.append(v)
            else:
                y = na_latent(h, P, o, cache_k[:, o], cache_v[:, o])
        x = x + g1 * y
        h = rmsnorm(x, P['norm_ffn_g'][i]) * (1 + sc2) + sh2
        x = x + g2 * conv_ffn(h, P, i)
    return rmsnorm(x, P['final_norm_g']), new_ssd, new_k, new_v

def setup_inputs(seed: int = 0) -> dict:
    key = jax.random.key(seed)
    ks = iter(jax.random.split(key, 40))

    def nrm(shape, s):
        return jax.random.normal(next(ks), shape, jnp.float32) * s

    dt0 = jnp.exp(jax.random.uniform(next(ks), (N_SSD_LAYERS, 2, SSD_HEADS), jnp.float32,
                                     np.log(1e-3), np.log(1e-1)))
    return {
        'x_prompt': nrm((BATCH, SEQ, D_MODEL), 1.0),
        'x_sample': nrm((DEC_BATCH, DEC_SEQ, D_MODEL), 1.0),
        'state_ssd': nrm((DEC_BATCH, N_SSD_LAYERS, 2, SSD_HEADS, SSD_HEADDIM, SSD_STATE), 0.5),
        'cache_k': nrm((DEC_BATCH, N_NA_LAYERS, PAST_LEN, NA_HEADS, NA_HEAD_DIM), 1.0),
        'cache_v': nrm((DEC_BATCH, N_NA_LAYERS, PAST_LEN, NA_HEADS, NA_HEAD_DIM), 1.0),
        'c': nrm((DEC_BATCH, D_MODEL), 1.0),
        'c_ctx': nrm((D_MODEL,), 1.0),
        'ada_w': nrm((DEPTH, D_MODEL, N_MOD * D_MODEL), 0.5 * D_MODEL ** -0.5),
        'ada_b': nrm((DEPTH, N_MOD * D_MODEL), 0.01),
        'norm_mix_g': 1.0 + nrm((DEPTH, D_MODEL), 0.02),
        'norm_ffn_g': 1.0 + nrm((DEPTH, D_MODEL), 0.02),
        'ssd_w_in': nrm((N_SSD_LAYERS, D_MODEL, MIX0_IN), D_MODEL ** -0.5),
        'ssd_conv_w': nrm((N_SSD_LAYERS, SSD_CONV_W, SSD_XBC), SSD_CONV_W ** -0.5),
        'ssd_conv_b': nrm((N_SSD_LAYERS, SSD_XBC), 0.01),
        'ssd_dt_bias': dt0 + jnp.log(-jnp.expm1(-dt0)),
        'ssd_a_log': jnp.log(jax.random.uniform(next(ks), (N_SSD_LAYERS, 2, SSD_HEADS), jnp.float32, 1.0, 16.0)),
        'ssd_d': 0.5 + nrm((N_SSD_LAYERS, 2, SSD_HEADS), 0.02),
        'ssd_norm_g': 1.0 + nrm((N_SSD_LAYERS, SSD_INNER), 0.02),
        'sc_conv_w': nrm((N_SSD_LAYERS, SC_CONV_W, SC_WIDTH), SC_CONV_W ** -0.5),
        'mix0_w_out': nrm((N_SSD_LAYERS, MIX0_OUT, D_MODEL), MIX0_OUT ** -0.5),
        'na_w_qkv': nrm((N_NA_LAYERS, D_MODEL, 3 * NA_INNER), D_MODEL ** -0.5),
        'na_rpb': nrm((N_NA_LAYERS, NA_HEADS, 2 * NA_KH - 1, 2 * NA_KW - 1), 0.02),
        'na_w_out': nrm((N_NA_LAYERS, NA_INNER, D_MODEL), NA_INNER ** -0.5),
        'ffn_w_gate': nrm((DEPTH, D_MODEL, D_FF), D_MODEL ** -0.5),
        'ffn_w_up': nrm((DEPTH, D_MODEL, D_FF), D_MODEL ** -0.5),
        'ffn_conv_w': nrm((DEPTH, FFN_CONV_W, D_FF), FFN_CONV_W ** -0.5),
        'ffn_w_down': nrm((DEPTH, D_FF, D_MODEL), D_FF ** -0.5),
        'final_norm_g': 1.0 + nrm((D_MODEL,), 0.02),
    }

def reference(x_prompt, x_sample, state_ssd, cache_k, cache_v, c, c_ctx, ada_w, ada_b, norm_mix_g, norm_ffn_g,
              ssd_w_in, ssd_conv_w, ssd_conv_b, ssd_dt_bias, ssd_a_log, ssd_d, ssd_norm_g, sc_conv_w, mix0_w_out,
              na_w_qkv, na_rpb, na_w_out, ffn_w_gate, ffn_w_up, ffn_conv_w, ffn_w_down, final_norm_g):
    P = {'ada_w': ada_w, 'ada_b': ada_b, 'norm_mix_g': norm_mix_g, 'norm_ffn_g': norm_ffn_g,
         'ssd_w_in': ssd_w_in, 'ssd_conv_w': ssd_conv_w, 'ssd_conv_b': ssd_conv_b, 'ssd_dt_bias': ssd_dt_bias,
         'ssd_a_log': ssd_a_log, 'ssd_d': ssd_d, 'ssd_norm_g': ssd_norm_g, 'sc_conv_w': sc_conv_w,
         'mix0_w_out': mix0_w_out, 'na_w_qkv': na_w_qkv, 'na_rpb': na_rpb, 'na_w_out': na_w_out,
         'ffn_w_gate': ffn_w_gate, 'ffn_w_up': ffn_w_up, 'ffn_conv_w': ffn_conv_w, 'ffn_w_down': ffn_w_down,
         'final_norm_g': final_norm_g}
    y_prompt, ssd_list, k_list, v_list = run_stream(x_prompt, c_ctx[None, :], P, True, None, None, None)
    new_state_ssd = jnp.stack(ssd_list, axis=1)
    new_cache_k = jnp.stack(k_list, axis=1)
    new_cache_v = jnp.stack(v_list, axis=1)
    y_sample, _, _, _ = run_stream(x_sample, c, P, False, state_ssd, cache_k, cache_v)
    return (y_prompt, y_sample, new_state_ssd, new_cache_k, new_cache_v)


_drawn_inputs = setup_inputs


def setup_inputs(seed=0):
    import zlib

    import numpy as np

    out = dict(_drawn_inputs(seed))
    spreads = {}
    factors = {'cache_k': 3.201,
     'cache_v': 2.703,
     'norm_ffn_g': 6.899,
     'ssd_conv_b': 3.521,
     'ssd_d': 8.0,
     'ssd_norm_g': 8.0,
     'na_rpb': 8.0,
     'final_norm_g': 3.097}
    for name, (base, spread) in spreads.items():
        noise = np.random.default_rng([zlib.crc32(name.encode()), seed]).standard_normal(out[name].shape)
        drawn = base * np.exp(spread * noise) if base else spread * noise
        out[name] = jnp.asarray(drawn.astype(out[name].dtype))
    for name, factor in factors.items():
        out[name] = (out[name] * factor).astype(out[name].dtype)
    return out
```

```python
from contextlib import ExitStack, contextmanager

import concourse.bass as bass
from concourse import mybir

F32 = mybir.dt.float32
F32R = mybir.dt.float32r
I32 = mybir.dt.int32
ALU = mybir.AluOpType
ACT = mybir.ActivationFunctionType
AX_X = mybir.AxisListType.X

P = 128
D = 1024
C = D // P
NCTX, NLAT = 128, 512
PAD = 4
LAT0 = NCTX + PAD
T = LAT0 + NLAT
HALF = T // 2
NB0 = HALF - LAT0
HEADS, HD, NS = 16, 64, 128
GROUPS = 2
LC = NLAT // P
NC = LC + 1
EPS = 1e-6
GRID_W = 64
ROWS = NLAT // GRID_W
QW, SPAN = 16, 32
QB = GRID_W // QW
DR, DC = 15, 31
TABW = 64
BIG = 1e30
MIX_STEPS = 11
FF = 2816
FC = FF // P
FA = 12
FB = FC - FA
KINDS = 5
K_DA, K_SUM, K_DT, K_END, K_DEC = range(KINDS)
RAW, RING, ADA = 2, 4, 2
MODS = 6
DEPTH = 2
OUT_ACT, OUT_DVE = (0, 2), (1, 3, 4)
UNITS = 2 * NC
SECS = DEPTH * MODS
ADA_N = 512

MIX_RING = "maamaamaaaam"
OUT_RING = "maamaamm"
IN_SLOTS = 12
MIX_SLOTS = 4 * C
OUT_SLOTS = 2 * C
QKV_SLOTS = 3 * C
NA_SLOTS = C
SLOT_IN = 0
SLOT_MIX = SLOT_IN + IN_SLOTS
SLOT_OUT = SLOT_MIX + len(MIX_RING) * C
FFN_SLOTS = 2 * FC + 2 * 2 * C
SLOT_FFN = [SLOT_OUT + len(OUT_RING) * C // 2, SLOT_OUT + len(OUT_RING) * C // 2 + FFN_SLOTS + QKV_SLOTS + NA_SLOTS]
ADA_MIX, ADA_OUT = MIX_RING.count("a"), OUT_RING.count("a")
SLOT_QKV = SLOT_FFN[0] + FFN_SLOTS
SLOT_NA = SLOT_QKV + QKV_SLOTS
ALL_SLOTS = SLOT_FFN[1] + FFN_SLOTS
TILE_MIX = IN_SLOTS
TILE_OUT = TILE_MIX + MIX_SLOTS
FFN_TILES = 2 * FC + 2 * C
TILE_FFN = [TILE_OUT + C, TILE_OUT + C + FFN_TILES + QKV_SLOTS + C]
TILE_QKV = TILE_FFN[0] + FFN_TILES
TILE_NA = TILE_QKV + QKV_SLOTS

U_Z, U_XS, U_BC, U_DT = 0, D, 2 * D, 2 * D + 2 * GROUPS * NS
U_BG = U_DT + 2 * HEADS
U_CG, U_XIN = U_BG + D, U_BG + 2 * D

R_C, R_CCTX, R_NMIX, R_NFFN, R_FIN, R_SNORM, R_CW, R_CB = 0, 8, 16, 32, 48, 56, 64, 100
R_ADAB, R_SCW = P, P + 96
R_FW = [2 * P, 3 * P]
XBC = 12

WIN = [32, 24, 8, 0]
BTYPE = [0, 1, 1, 2]
TSTART = [0, 8, 16]


class Steps:

    def __init__(self, eng, sem):
        self.eng, self.sem, self.base, self.n = eng, sem, 0, 0

    def did(self, ins):
        ins.then_inc(self.sem, 1)
        self.n += 1

    def wait(self):
        self.eng.wait_ge(self.sem, self.base + self.n)

    def then_wait(self, ins):
        self.did(ins)
        self.wait()

    @contextmanager
    def loop(self, count, per):
        start = self.base + self.n
        with self.eng.Fori(0, count) as i:
            self.base, self.n = start + i * per, 0
            yield i
            assert self.n == per, f"steps per iteration: {self.n}"
        self.base, self.n = start + count * per, 0


def trunk(nc, x_prompt, x_sample, state_ssd, cache_k, cache_v, c, c_ctx, ada_w, ada_b, norm_mix_g, norm_ffn_g,
          ssd_w_in, ssd_conv_w, ssd_conv_b, ssd_dt_bias, ssd_a_log, ssd_d, ssd_norm_g, sc_conv_w, mix0_w_out,
          na_w_qkv, na_rpb, na_w_out, ffn_w_gate, ffn_w_up, ffn_conv_w, ffn_w_down, final_norm_g,
          y_prompt, y_sample, new_state, new_k, new_v):
    x_dram = nc.dram_tensor("x_spill", [P, C * T], F32, kind="Internal").ap()
    tab_dram = nc.dram_tensor("bias_table", [HEADS, DR * TABW], F32, kind="Internal").ap()

    with ExitStack() as ctx:
        def sb(name, shape, dt=F32):
            return ctx.enter_context(nc.sbuf_tensor(name, shape, dt))

        def sem(name):
            return ctx.enter_context(nc.semaphore(name))

        raw = sb("raw", [P, RAW, C * P])
        w_hi = sb("w_hi", [P, RING, C * P], F32R)
        first_lo_at = -(-nc.sbuf_base // 32) * 32
        w_lo = sb("w_lo", [P, RING, C * P], F32R)
        assert nc.sbuf_base == first_lo_at + RING * C * P * 4, (nc.sbuf_base, first_lo_at)
        act_hi = sb("act_hi", [P, C * T], F32R)
        outs_at = -(-nc.sbuf_base // 32) * 32
        act_lo = sb("act_lo", [P, C * T], F32R)
        assert nc.sbuf_base == outs_at + C * T * 4, (nc.sbuf_base, outs_at)
        ident = sb("ident", [P, P])
        ones = sb("ones", [P, P])
        eps = sb("eps", [P, 2])
        zeros = sb("zeros", [P, C * PAD])
        tri = sb("tri", [P, 4, P])
        par = sb("par", [P, 4 * P])
        halfw = sb("halfw", [P, 48])
        csil = sb("csil", [P, C, 2])
        csil_r = sb("csil_r", [P, C, 4], F32R)
        sel = sb("sel", [4, 2])
        csth = sb("csth", [P, 2, C])
        mod = sb("mod", [P, DEPTH * MODS, C, 2])
        scale_a = sb("scale_a", [P, C, 2])
        dskip = sb("dskip", [P, C])
        dld = sb("dld", [P, 2, HEADS])
        qi = sb("qi", [P, 1 + SPAN], I32)
        qf = sb("qf", [P, 4 + 3 * SPAN])
        masks = sb("masks", [P, 3, SPAN])
        dtb = sb("dtb", [P, 2, 2 * HEADS])
        at_base = -(-nc.sbuf_base // 32) * 32
        arena_bytes = nc.sbuf_top - at_base

        def at(name, off, shape, dt=F32):
            n = 4
            for s in shape[1:]:
                n *= s
            assert off + n <= arena_bytes, (name, off + n, arena_bytes)
            return nc.alloc_sbuf_tensor_at(name, shape, dt, offset=at_base + off)

        CT = C * T * 4
        X0 = 2 * CT + 4 * T * 4
        x = at("x", X0, [P, C * T])
        AFTER = X0 + CT
        ROW = 2592

        tok = at("tok", 0, [P, NC, D])
        prow = at("prow", 5 * D * 4, [P, 4, P])
        tabr = at("tabr", 5 * D * 4 + 2048, [HEADS, DR, DC])
        tab = at("tab", 5 * D * 4 + 2048 + 1888, [HEADS, DR, TABW])
        rms = at("rms", AFTER, [P, T])
        rinv = at("rinv", AFTER + ROW, [P, T])
        nt = at("nt", AFTER + 2 * ROW, [P, 2, T])
        N0 = 108032
        acc = at("acc", N0, [P, T])
        sq = at("sq", N0 + ROW, [P, T])
        arow = at("arow", N0 + ROW, [4, ADA_N])
        frow = at("frow", 0, [2, 2 * D])
        first_at = [2 * CT, AFTER + 4 * ROW, AFTER + 4 * ROW + 8192, AFTER + 4 * ROW + 16384,
                    (arena_bytes - ADA * C * P * 4) // 32 * 32]
        first = [at(f"first{n}", o, [P, C, 2 * P]) for n, o in enumerate(first_at)]
        first += [nc.alloc_sbuf_tensor_at(f"first{5 + n}", [P, C, 2 * P], F32, offset=first_lo_at + n * 2 * C * P * 4) for n in range(2)]

        xs = at("xs", 0, [P, C * T])
        xs_lo = at("xs_lo", 0, [P, C * T], F32R)
        yb = at("yb", CT, [P, C * T])
        yb_lo = at("yb_lo", CT, [P, C * T], F32R)
        bc = at("bc", 2 * CT, [P, 4, T])
        o = [X0]

        def mix(name, shape, dt=F32):
            n = 4
            for s in shape[1:]:
                n *= s
            t = at(name, o[0], shape, dt)
            o[0] += (n + 31) // 32 * 32
            return t

        ada = at("ada", (arena_bytes - ADA * C * P * 4) // 32 * 32, [P, ADA, C * P])
        mbuf = mix("mbuf", [P, 5, NLAT])
        cs = mix("cs", [P, 4, NLAT])
        xdw = mix("xdw", [P, 4, NC, P])
        hin = mix("hin", [P, 2, LC, P])
        gm = mix("gm", [P, 2, NC * P])
        btok = mix("btok", [P, NC, NS])
        h0 = mix("h0", [P, 2, NS])
        xsj = mix("xsj", [P, T])
        zs = mix("zs", [P, T])
        cgs = mix("cgs", [P, T])
        gpad = mix("gpad", [P, T + 2])
        sc = mix("sc", [P, NC, KINDS, 2 * HEADS])
        col = mix("col", [P, NC * KINDS, 2, 2])
        sto = mix("sto", [P, 2, NS])
        wdt = at("wdt", CT + 10240, [P, C, 32])
        wdt_hi = at("wdt_hi", CT + 11264, [P, C, 32], F32R)
        wdt_lo = at("wdt_lo", CT + 12288, [P, C, 32], F32R)
        dtt = at("dtt", CT + 13312, [P, 6, NC * 32])
        dtrow = at("dtrow", CT + 17152, [2 * HEADS, T])

        f_hi = at("f_hi", 0, [P, FA * T], F32R)
        f_lo = at("f_lo", AFTER, [P, FA * T], F32R)
        fo = AFTER + FA * T * 4
        fg = [at("fg0", FA * T * 4, [P, T + 2]), at("fg1", FA * T * 4 + ROW, [P, T + 2])]
        ft = [at("ft0", FA * T * 4 + 2 * ROW, [P, T]), at("ft1", FA * T * 4 + 3 * ROW, [P, T])]
        fe = [at("fe0", FA * T * 4 + 4 * ROW, [P, T]), at("fe1", FA * T * 4 + 5 * ROW, [P, T])]
        fa = [at("fa0", FA * T * 4 + 6 * ROW, [P, T]), at("fa1", fo, [P, T])]

        TQ = NLAT + NCTX
        kt = at("kt", 0, [P, C * TQ])
        qt = at("qt", C * TQ * 4, [P, C * TQ])
        vwin = at("vwin", 2 * C * TQ * 4, [P, 8 * P])
        sbf = at("sbf", 2 * C * TQ * 4, [P, 2, 384])
        kct = at("kct", 2 * C * TQ * 4 + 2 * TQ * 4, [P, C * P])
        ao = [X0]

        def na(name, shape, dt=F32):
            n = 4
            for s in shape[1:]:
                n *= s
            t = at(name, ao[0], shape, dt)
            ao[0] += (n + 31) // 32 * 32
            return t

        bias = na("bias", [P, 2, 3, 384])
        vs = na("vs", [P, TQ])
        qz = na("qz", [P, 2, TQ])
        kx = na("kx", [P, P])
        ot = na("ot", [P, NC, P])
        sums = na("sums", [P, 2, NC])
        nmax = na("nmax", [P, 2])
        rsum = na("rsum", [P, 2, NC])
        win = na("win", [P, 2, ROWS, 48])
        vtok = na("vtok", [P, 8, D])
        vc = na("vc", [P, D])
        kc = na("kc", [P, D])
        pbf = na("pbf", [P, 2, 384])
        ptb = na("ptb", [P, 2, 384])
        outs = nc.alloc_sbuf_tensor_at("outs", [P, NC, D], F32, offset=outs_at)
        gx = at("gx", N0 + 2 * ROW, [P, 2, T])
        root_t = at("root_t", N0 + 4 * ROW, [P, NC, 2])
        rinv_t = at("rinv_t", N0 + 4 * ROW + 64, [P, NC, 2])

        ps = ctx.enter_context(nc.psum_tensor("ps", [P, 8, 512], F32))

        S = {n: sem(n) for n in (
            "raw_loaded0 raw_loaded1 high_split low_split slot_used tile_free0 tile_free1 "
            "params_loaded tokens_loaded table_loaded table_stored consts_ready table_ready dskip_loaded "
            "par_transposed par_ready first_loaded0 first_loaded1 first_loaded2 first_loaded3 first_loaded4 first_loaded5 first_loaded6 first_loaded7 dtrow_ready ya_ready csil_ready x_transposed x_copied ada_loaded0 ada_loaded1 ada_used csil_high row_copied mod_turned first_summed first_copied first_turned "
            "mod_summed mod_ready squares_ready squares_used squares_summed rms_ready scaled_ready act_high "
            "act_ready x_spilled x_reloaded wdt_loaded wdt_ready dt_summed sc_ready sums_ready "
            "group_summed group_ready prep_ready xtok_ready xtok_taken ctok_ready "
            "ctok_taken rows_ready rows_exp seg_ready seg_exp m_ready hf_ready hf_taken hb_ready hb_taken y_ready "
            "y_taken cstate_ready cstate_taken cstate_stored h0_loaded gate_tanh csil_tanh sums_exp dt_exp a_exp wdt_high yb_high xin_ready conv_scaled "
            "conv_ready conv_tanh ffn_conv ffn_gelu ffn_ready ffn_high yb_ready "
            "q_taken v_windowed v_transposed v_taken caches_loaded kc_transposed kc_ready attn_copied scores_ready "
            "scores_taken probs_ready pt_ready pt_copied o_ready o_taken o_transposed o_high o_low win_loaded0 "
            "win_loaded1 bias_ready bias_used gx_ready gx_turned out_copied token_sums token_roots out_scaled stored k_stored dve act pool").split()}

        V = lambda s: ps[:, 2 * s:2 * s + 2, 0:HALF]
        F = lambda a: a.rearrange("p (b n) -> p b n", b=2)
        PIECES = [(0, 0, NCTX, 0, 1), (0, LAT0, HALF, LAT0, 0), (1, 0, HALF, HALF, 0)]
        STREAMS = [(0, NCTX, 1), (LAT0, T, 0)]

        block = ctx.enter_context(nc.Block())

        def slot16(b, i, s):
            n = b - (ADA_MIX * C + ADA_OUT * C // 2 if b >= SLOT_FFN[0] else 0) + s
            return 16 * (n // RAW + 1) + 16 * (4 // RAW) * i

        def ring_slot(ring, mains, adas, i, t):
            kinds = ring + ring
            n = kinds[:t].count(kinds[t])
            per = ring.count(kinds[t])
            if kinds[t] == "m":
                return raw[:, n % RAW], S[f"raw_loaded{n % RAW}"], 16 * ((mains + n) // RAW + 1) + 16 * per // RAW * i
            return ada[:, n % ADA], S[f"ada_loaded{n % ADA}"], 16 * ((adas + n) // ADA + 1) + 16 * per // ADA * i

        def mix_slot(j, t):
            return ring_slot(MIX_RING, IN_SLOTS, 0, j, t)

        def out_slot(i, t):
            return ring_slot(OUT_RING, IN_SLOTS + MIX_SLOTS, ADA_MIX * C, i, t)

        def rows(dram, k0, k1, col):
            return dram.rearrange("(k p) n -> p k n", p=P)[:, k0:k1, bass.ds(col, P)]

        w_in, w_out = ssd_w_in[0], mix0_w_out[0]
        w_qkv, w_no = na_w_qkv[0], na_w_out[0]
        FPARTS = [(0, FA), (FA, FB)]

        @block.sync
        def _(sp):
            def weights(b, i, s, src, nk=C):
                if not (isinstance(i, int) and b + 4 * i + s < RAW):
                    sp.wait_ge(S["low_split"], b + s - RAW + 1 + 4 * i)
                dst = raw[:, s % RAW, 0:nk * P].rearrange("p (k n) -> p k n", k=nk)
                sp.dma_start(dst, src).then_inc(S[f"raw_loaded{s % RAW}"], 16)

            def params(tile_row, src):
                t, r = tile_row // P, tile_row % P
                n = src.shape[0]
                sp.dma_start(prow[r:r + n, t, :], src).then_inc(S["params_loaded"], 16)

            k_p = "a (k p) -> (a k) p"
            params(R_C, c.rearrange(k_p, p=P))
            params(R_CCTX, c_ctx.rearrange("(k p) -> k p", p=P))
            params(R_NMIX, norm_mix_g.rearrange(k_p, p=P))
            params(R_NFFN, norm_ffn_g.rearrange(k_p, p=P))
            params(R_FIN, final_norm_g.rearrange("(k p) -> k p", p=P))
            params(R_SNORM, ssd_norm_g.rearrange(k_p, p=P))
            params(R_CW, ssd_conv_w[0].rearrange(k_p, p=P))
            params(R_CB, ssd_conv_b.rearrange(k_p, p=P))
            params(R_ADAB, ada_b.rearrange(k_p, p=P))
            params(R_SCW, sc_conv_w[0].rearrange(k_p, p=P))
            for lay in range(DEPTH):
                params(R_FW[lay], ffn_conv_w[lay].rearrange(k_p, p=P))
            sp.dma_start(tok[:, 0:LC, :], x_sample[0].rearrange("(c p) d -> p c d", p=P)).then_inc(S["tokens_loaded"], 16)
            sp.dma_start(tok[:, LC, :], x_prompt[0]).then_inc(S["tokens_loaded"], 16)
            for n in range(C):
                if n >= len(first):
                    sp.wait_ge(S["first_summed"], n - len(first) + 1)
                sp.dma_start(first[n % len(first)][:], ada_w[0].rearrange("(k p) n -> p k n", p=P)[:, :, 2 * n * P:2 * n * P + 2 * P]
                             ).then_inc(S[f"first_loaded{n}"], 16)
            for s in range(RAW):
                weights(SLOT_IN, 0, s, rows(w_in, 0, C, U_BC + s * P))
            sp.dma_start(wdt[:], w_in.rearrange("(k p) n -> p k n", p=P)[:, :, U_DT:U_DT + 2 * HEADS]
                         ).then_inc(S["wdt_loaded"], 16)
            all_partitions = [[0, P], [1, 2 * HEADS]]
            for n, v in enumerate((ssd_dt_bias, ssd_a_log)):
                sp.dma_start(dtb[:, n, :], bass.AP(tensor=v.tensor, offset=0, ap=all_partitions)
                             ).then_inc(S["dskip_loaded"], 16)
            sp.dma_start(dld[:].rearrange("p a h -> p (a h)"), bass.AP(tensor=ssd_d.tensor, offset=0, ap=all_partitions)
                         ).then_inc(S["dskip_loaded"], 16)
            sp.dma_start(tabr[:], na_rpb[0]).then_inc(S["table_loaded"], 16)
            sp.wait_ge(S["x_copied"], C)
            sp.dma_start(x_dram, x[:]).then_inc(S["x_spilled"], 16)
            for s in range(RAW, 4):
                weights(SLOT_IN, 0, s, rows(w_in, 0, C, U_BC + s * P))
            with sp.Fori(0, 2) as i:
                for s in range(4):
                    weights(SLOT_IN + 4, i, s, rows(w_in, 0, C, U_XS + (4 * i + s) * P))
            MIXW = [U_Z, U_CG, U_XIN, U_BG]

            def ring_load(slot, base, ring, i, t, src):
                dst, loaded, _ = slot
                kinds = ring + ring
                back = [q for q in range(t + len(ring)) if kinds[q] == ring[t]][-2]
                if isinstance(i, int) and i == 0 and back < len(ring):
                    if base == SLOT_MIX and ring[t] == "m":
                        sp.wait_ge(S["low_split"], SLOT_MIX - RAW + ring[:t].count("m") + 1)
                    elif base == SLOT_MIX:
                        sp.wait_ge(S["first_summed"], C)
                    else:
                        sp.wait_ge(S["low_split"], base - 1 if ring[t] == "m" or t == 1 else base)
                else:
                    sp.wait_ge(S["low_split"], base + back - len(ring) + 1 + len(ring) * i)
                k = C if ring[t] == "m" else 2
                sp.dma_start(dst.rearrange("p (k n) -> p k n", k=k), src).then_inc(loaded, 16)

            def ada_rows(lay, col, k):
                wide = MODS * D
                return bass.AP(tensor=ada_w.tensor, offset=col + (lay * D + 2 * k * P) * wide, ap=[[wide, P], [P * wide, 2], [1, ADA_N]])

            def mix_loads(j, lay, sec):
                for t, kind in enumerate(MIX_RING):
                    n = MIX_RING[:t].count(kind)
                    src = rows(w_in, 0, C, MIXW[n] + j * P) if kind == "m" else ada_rows(lay, sec * D + n // 4 * ADA_N, n % 4)
                    ring_load(mix_slot(j, t), SLOT_MIX, MIX_RING, j, t, src)


            def state_of(j):
                return bass.AP(tensor=state_ssd.tensor, offset=j * (P * NS), ap=[[NS, P], [HEADS * HD * NS, 2], [1, NS]])

            def state_load(src):
                sp.dma_start(h0[:], src).then_inc(S["h0_loaded"], 16)

            sp.wait_ge(S["x_spilled"], 16)
            sp.wait_ge(S["act_ready"], C)
            state_load(state_of(0))
            sp.wait_ge(S["table_ready"], 1)
            sp.dma_start(tab_dram, tab[:].rearrange("h r c -> h (r c)")).then_inc(S["table_stored"], 16)
            mix_loads(0, 0, 2)

            for lay, j0, j1, sec0 in ((0, 1, MODS - 2, 2), (1, MODS - 2, C, 2 - MODS)):
                with sp.Fori(j0, j1) as j:
                    src = state_of(j)
                    sp.wait_ge(S["ctok_ready"], j)
                    state_load(src)
                    mix_loads(j, lay, j + sec0)

            def out_loads(i):
                for t, kind in enumerate(OUT_RING):
                    n = OUT_RING[:t].count(kind)
                    half = w_out[D:2 * D] if n < 2 else w_out[0:D]
                    src = rows(half, 0, C, (2 * i + n % 2) * P) if kind == "m" else ada_rows(1, (MODS - 2) * D + i * ADA_N, n)
                    ring_load(out_slot(i, t), SLOT_OUT, OUT_RING, i, t, src)

            for i in range(C // 2):
                out_loads(i)

            def ffn_loads(lay):
                b = SLOT_FFN[lay]
                for f0, nf in FPARTS:
                    with sp.Fori(0, nf // 2) as i:
                        for s in range(4):
                            w = (ffn_w_gate, ffn_w_up)[s % 2][lay]
                            weights(b, i, s, rows(w, 0, C, (f0 + s // 2 + 2 * i) * P))
                    b += 2 * nf
                    with sp.Fori(0, C // 2) as i:
                        for s in range(4):
                            k0 = f0 + (s % 2) * nf // 2
                            weights(b, i, s, rows(ffn_w_down[lay], k0, k0 + nf // 2, (2 * i + s // 2) * P), nf // 2)
                    b += 2 * C

            ffn_loads(0)
            QKV = [2 * D, D, 0]
            for s in range(4):
                weights(SLOT_QKV, 0, s, rows(w_qkv, 0, C, QKV[0] + s * P))
            for s in range(2):
                sp.wait_ge(S[f"tile_free{s}"], TILE_QKV // 2)
            sp.dma_start(x_dram, x[:]).then_inc(S["x_spilled"], 16)

            def windows_of(h):
                return [bass.AP(tensor=tab_dram.tensor, offset=h * (DR * TABW) + r * TABW, ap=[[1, QW], [TABW, ROWS], [1, 48]])
                        for r in range(ROWS)]

            def window_load(hh, windows):
                for r in range(ROWS):
                    sp.dma_start(win[QW * r:QW * r + QW, hh], windows[r]).then_inc(S[f"win_loaded{hh}"], 16)

            sp.wait_ge(S["act_ready"], 4 * C)
            sp.wait_ge(S["x_spilled"], 32)
            sp.wait_ge(S["table_stored"], 16)
            sp.dma_start(kc[:], cache_k[0, 0].rearrange("s h d -> s (h d)")).then_inc(S["caches_loaded"], 16)
            sp.dma_start(vc[:], cache_v[0, 0].rearrange("s h d -> s (h d)")).then_inc(S["caches_loaded"], 16)
            for hh in range(2):
                window_load(hh, windows_of(hh))
            for part in range(3):
                b = SLOT_QKV + part * C
                with sp.Fori(1 if part == 0 else 0, 2) as i:
                    for s in range(4):
                        weights(b, i, s, rows(w_qkv, 0, C, QKV[part] + (4 * i + s) * P))
            for s in range(4):
                weights(SLOT_NA, 0, s, rows(w_no, 0, C, s * P))
            with sp.Fori(0, C - 1) as i:
                for hh in range(2):
                    windows = windows_of(2 * i + 2 + hh)
                    sp.wait_ge(S["bias_ready"], 2 * i + hh + 1)
                    window_load(hh, windows)
            sp.wait_ge(S["o_low"], C + 1)
            sp.wait_ge(S["k_stored"], 32)
            sp.dma_start(x[:], x_dram).then_inc(S["x_reloaded"], 16)
            for s in range(4):
                weights(SLOT_NA + 4, 0, s, rows(w_no, 0, C, (4 + s) * P))
            ffn_loads(1)
            for q, n in enumerate(OUT_DVE):
                sp.wait_ge(S["out_scaled"], q + 1)
                dst = y_sample[0, n * P:n * P + P, :] if n < LC else y_prompt[0]
                sp.dma_start(dst, outs[:, n, :]).then_inc(S["stored"], 16)

        @block.gpsimd
        def _(pool):
            st = Steps(pool, S["pool"])
            g = nc.gpsimd
            st.did(g.memset(ident[:], 0.0))
            st.did(g.memset(ones[:], 1.0))
            st.did(g.memset(eps[:], EPS))
            st.did(g.memset(zeros[:], 0.0))
            st.did(g.memset(tri[:], 1.0))
            st.wait()
            g.affine_select(out=ident[:], in_=ident[:], compare_op=ALU.not_equal, fill=1.0, base=0, pattern=[[-1, P]], channel_multiplier=1)
            for n, (op, sign) in enumerate(((ALU.is_ge, 1), (ALU.is_ge, -1), (ALU.is_gt, 1), (ALU.is_gt, -1))):
                last = g.affine_select(out=tri[:, n, :], in_=tri[:, n, :], compare_op=op, fill=0.0, base=0,
                                       pattern=[[sign, P]], channel_multiplier=-sign)
            last.then_inc(S["consts_ready"], 1)
            g.iota(qi[:, 0:1], pattern=[[0, 1]], base=0, channel_multiplier=1)
            g.iota(qi[:, 1:1 + SPAN], pattern=[[1, SPAN]], base=0, channel_multiplier=0).then_inc(S["consts_ready"], 1)

            def low(b, i, s):
                pool.wait_ge(S["high_split"], b + s + 1 + 4 * i)
                g.tensor_tensor(w_lo[:, s], raw[:, s % RAW], w_hi[:, s], ALU.subtract).then_inc(S["low_split"], 1)

            def ring_low(slot, base, ring, i, t):
                pool.wait_ge(S["high_split"], base + t + 1 + len(ring) * i)
                g.tensor_tensor(w_lo[:, t % RING], slot[0], w_hi[:, t % RING], ALU.subtract).then_inc(S["low_split"], 1)

            with pool.Fori(0, IN_SLOTS // 4) as i:
                for s in range(4):
                    low(0, i, s)
            with pool.Fori(0, C) as j:
                for t in range(len(MIX_RING)):
                    ring_low(mix_slot(j, t), SLOT_MIX, MIX_RING, j, t)
            with pool.Fori(0, C // 2) as i:
                for t in range(len(OUT_RING)):
                    ring_low(out_slot(i, t), SLOT_OUT, OUT_RING, i, t)
            with pool.Fori(0, (SLOT_NA - SLOT_FFN[0]) // 4) as i:
                for s in range(4):
                    low(SLOT_FFN[0], i, s)
            pool.wait_ge(S["x_spilled"], 32)
            for s in range(4):
                low(SLOT_NA, 0, s)
            pool.wait_ge(S["attn_copied"], 1)
            with pool.Fori(0, C) as i:
                for hh in range(2):
                    pool.wait_ge(S[f"win_loaded{hh}"], 128 * i + 128)
                    pool.wait_ge(S["bias_used"], 2 * i + hh + 1)
                    for t in range(3):
                        dst = bias[:, hh, t, 0:256].rearrange("p (k r c) -> p k r c", k=2, r=ROWS)
                        w = win[:, hh, :, TSTART[t]:TSTART[t] + SPAN].rearrange("p r (k c) -> p k r c", k=2)
                        m = masks[:, t, :].rearrange("p (k c) -> p k c", k=2).unsqueeze(2).broadcast_to([P, 2, ROWS, QW])
                        last = g.tensor_tensor(dst, w, m, ALU.add)
                    last.then_inc(S["bias_ready"], 1)
            with pool.Fori(0, (ALL_SLOTS - SLOT_NA - 4) // 4) as i:
                for s in range(4):
                    low(SLOT_NA + 4, i, s)

        def chunk_of(buf, k, cols=slice(0, T)):
            return buf[:, k * T + cols.start:k * T + cols.stop]

        @block.tensor
        def _(pe):
            t = t_ = nc.tensor

            def half_slot(tset, s, ks, src_hi, src_lo, first, last, k0=0, before=None):
                for k in ks:
                    if before is not None:
                        pe.wait_ge(S[before[0]], before[1] + k)
                    hi, lo = w_hi[:, s, k * P:k * P + P], w_lo[:, s, k * P:k * P + P]
                    start, stop = first and k == ks[0], last and k == ks[-1]
                    for h in range(2):
                        cols = slice(h * HALF, h * HALF + HALF)
                        out = ps[:, 2 * tset + h, 0:HALF]
                        t.matmul(out, hi, chunk_of(src_hi, k0 + k, cols), start=start, stop=False)
                        t.matmul(out, hi, chunk_of(src_lo, k0 + k, cols), start=False, stop=False)
                    for h in range(2):
                        cols = slice(h * HALF, h * HALF + HALF)
                        mm = t.matmul(ps[:, 2 * tset + h, 0:HALF], lo, chunk_of(src_hi, k0 + k, cols), start=False, stop=stop)
                return mm

            def slot_ready(b, i, s):
                pe.wait_ge(S["low_split"], b + s + 1 + 4 * i)

            def tile_free(tb, per, i, k):
                n = tb + k
                if not (isinstance(i, int) and n + per * i < 2):
                    pe.wait_ge(S[f"tile_free{k % 2}"], n // 2 + (per // 2) * i)

            def whole_tile(b, i, s, tb, per, k, norm=None):
                slot_ready(b, i, s)
                tile_free(tb, per, i, k)
                before = ("act_ready", C * norm + 1) if norm is not None and s == 0 else None
                half_slot(k % 2, s, range(C), act_hi, act_lo, True, True, before=before).then_inc(S["slot_used"], 1)

            def norm_stats(n):
                bank = 2 if n == 0 else 6
                if n == 1:
                    pe.wait_ge(S["mod_ready"], 1 + C)
                pe.wait_ge(S["squares_used"], C * (n + 1))
                for b in range(2):
                    mm = t.matmul(ps[:, bank + b, 0:HALF], ones[:], acc[:, b * HALF:b * HALF + HALF], start=True, stop=True)
                mm.then_inc(S["squares_summed"], 1)

            def act_ready(n):
                pe.wait_ge(S["act_ready"], n)

            def ada_tile(bank, base, per, i, t, n):
                pe.wait_ge(S["low_split"], base + t + 1 + per * i)
                for k in range(2):
                    for w, last in ((w_hi, False), (w_lo, True)):
                        mm = t_.matmul(ps[0:4, bank, :], csil_r[:, 2 * n + k, :], w[:, t % RING, k * ADA_N:k * ADA_N + ADA_N],
                                       start=(n == 0 and k == 0 and not last), stop=(n == 3 and k == 1 and last))
                mm.then_inc(S["slot_used"], 1)
                return mm

            def ada_columns(bank, col):
                for n in range(ADA_N // P):
                    mm = t_.matmul(ps[:, bank, col + 2 * n:col + 2 * n + 2], arow[:, n * P:n * P + P], sel[:], start=True, stop=True)
                mm.then_inc(S["mod_turned"], 1)

            pe.wait_ge(S["consts_ready"], 2)
            pe.wait_ge(S["params_loaded"], 16 * 12)
            for n, r in enumerate((112, 120, 3 * FC, 3 * FC)):
                mm = t.transpose(ps[:, 4, n * P:n * P + r], prow[0:r, n, :], ident[0:r, 0:r])
            mm.then_inc(S["par_transposed"], 1)
            pe.wait_ge(S["csil_ready"], 1)
            pe.wait_ge(S["tokens_loaded"], 32)
            for s in range(C):
                if s >= 2:
                    pe.wait_ge(S["x_copied"], s - 1)
                for n in range(LC):
                    t.transpose(ps[:, 5 + s % 2, n * P:n * P + P], tok[:, n, s * P:s * P + P], ident[:])
                t.transpose(ps[:, s % 2, 0:P], tok[:, LC, s * P:s * P + P], ident[:]).then_inc(S["x_transposed"], 1)
            FIRST_BANKS = [7, 4, 0, 1]

            def first_columns(n):
                pe.wait_ge(S["first_copied"], n + 1)
                for q in range(4 * n, 4 * n + 4):
                    mm = t.matmul(ps[:, 5, 2 * q:2 * q + 2], frow[:, q * P:q * P + P], ident[0:2, 0:2], start=True, stop=True)
                mm.then_inc(S["first_turned"], 1)

            pe.wait_ge(S["x_copied"], C)
            for n in range(C):
                pe.wait_ge(S[f"first_loaded{n}"], 16)
                for k in range(C):
                    mm = t.matmul(ps[0:2, FIRST_BANKS[n // 2], n % 2 * 2 * P:n % 2 * 2 * P + 2 * P], csil[:, k, :], first[n % len(first)][:, k, :],
                                  start=(k == 0), stop=(k == C - 1))
                mm.then_inc(S["first_summed"], 1)
                if n == C // 2:
                    norm_stats(0)
                if n % 2 == 1 and n > 1:
                    first_columns(n // 2 - 1)
            first_columns(C // 2 - 1)

            pe.wait_ge(S["wdt_ready"], 1)
            pe.wait_ge(S["mod_ready"], 1)
            for k in range(C):
                pe.wait_ge(S["act_ready"], k + 1)
                for h in range(2):
                    out, cols = ps[0:2 * HEADS, 5 + h, 0:HALF], slice(h * HALF, h * HALF + HALF)
                    t.matmul(out, wdt_hi[:, k, :], chunk_of(act_hi, k, cols), start=(k == 0), stop=False)
                    t.matmul(out, wdt_hi[:, k, :], chunk_of(act_lo, k, cols), start=False, stop=False)
                    mm = t.matmul(out, wdt_lo[:, k, :], chunk_of(act_hi, k, cols), start=False, stop=(k == C - 1))
            mm.then_inc(S["dt_summed"], 1)
            pe.wait_ge(S["rms_ready"], 1)
            whole_tile(SLOT_IN, 0, 0, 0, 4, 0)
            pe.wait_ge(S["dtrow_ready"], 1)
            for n in range(NC):
                c0 = LAT0 + n * P if n < LC else 0
                mm = t.transpose(ps[:, 5, n * 32:n * 32 + 32], dtrow[:, c0:c0 + P], ident[0:2 * HEADS, 0:2 * HEADS])
            mm.then_inc(S["dt_summed"], 1)
            for s in range(1, 4):
                whole_tile(SLOT_IN, 0, s, 0, 4, s)
            pe.wait_ge(S["sc_ready"], 1)
            for n in range(NC):
                f, bwd = sc[:, n, K_DA, 0:HEADS], sc[:, n, K_DA, HEADS:2 * HEADS]
                for q, (lhs, rhs) in enumerate(((tri[:, 0, :], f), (tri[:, 1, :], bwd), (tri[:, 3, :], f), (tri[:, 2, :], bwd))):
                    t.matmul(ps[:, 6, n * 96 + q * HEADS:n * 96 + q * HEADS + HEADS], lhs, rhs, start=True, stop=True)
                mm = t.matmul(ps[:, 6, n * 96 + 64:n * 96 + 96], ones[:], sc[:, n, K_DA, :], start=True, stop=True)
            mm.then_inc(S["sums_ready"], 1)
            with pe.Fori(0, 2) as i:
                for s in range(4):
                    whole_tile(SLOT_IN + 4, i, s, 4, 4, s)

            def rows_of(u):
                for n in range(LC):
                    lhs = col[:, n * KINDS + K_DA, u % 2, u // 2:u // 2 + 1].broadcast_to([P, P])
                    mm = t.matmul(ps[:, 5, n * P:n * P + P], lhs, tri[:, u % 2, :], start=True, stop=True)
                mm.then_inc(S["rows_ready"], 1)

            for g in range(GROUPS):
                pe.wait_ge(S["mod_ready"], 1 + (C // GROUPS) * g)
                pe.wait_ge(S["xin_ready"], IN_SLOTS)
                for n in range(NC):
                    c0 = LAT0 + n * P if n < LC else 0
                    bank, off = (5, n * P) if n < LC else (7, 0)
                    t.matmul(ps[:, bank, off:off + P], bc[:, g, c0:c0 + P], bc[:, 2 + g, c0:c0 + P], start=True, stop=True)
                    bank = 6 if n < LC else 4
                    mm = t.transpose(ps[:, bank, off:off + P], bc[:, g, c0:c0 + P], ident[:])
                mm.then_inc(S["group_summed"], 1)
                pe.wait_ge(S["group_ready"], g + 1)
                j0 = (C // GROUPS) * g
                with pe.Fori(0, C // GROUPS) as i:
                    MAIN = [t for t, kind in enumerate(MIX_RING) if kind == "m"]
                    base = SLOT_MIX + len(MIX_RING) * j0

                    def gemm_half(s, h):
                        if h == 0:
                            pe.wait_ge(S["low_split"], base + MAIN[s] + 1 + len(MIX_RING) * i)
                            tile_free(TILE_MIX + 4 * j0, 4, i, s)
                        mm = half_slot(s % 2, MAIN[s] % RING, range(4 * h, 4 * h + 4), act_hi, act_lo, h == 0, h == 1)
                        if h == 1:
                            mm.then_inc(S["slot_used"], 1)

                    def section(n):
                        if n == 4:
                            pe.wait_ge(S["row_copied"], 2 * (j0 + i) + 1)
                        t_slot = [t for t, kind in enumerate(MIX_RING) if kind == "a"][n]
                        ada_tile(7, base, len(MIX_RING), i, t_slot, n % 4)

                    def bank5_free(n):
                        pe.wait_ge(S["seg_ready"], 5 * (j0 + i) + n)

                    gemm_half(0, 0)
                    pe.wait_ge(S["prep_ready"], j0 + i + 1)
                    for n in range(LC):
                        mm = t.transpose(ps[:, 4, n * P:n * P + P], xsj[:, LAT0 + n * P:LAT0 + n * P + P], ident[:])
                    mm.then_inc(S["xtok_ready"], 1)
                    rows_of(0)
                    gemm_half(0, 1)
                    section(0)
                    section(1)
                    bank5_free(1)
                    rows_of(1)
                    pe.wait_ge(S["xtok_taken"], j0 + i + 1)
                    t.transpose(ps[:, 4, 0:P], xsj[:, 0:NCTX], ident[:])
                    pe.wait_ge(S["h0_loaded"], 16 * (j0 + i) + 16)
                    t.transpose(ps[:, 4, P:2 * P], h0[:, 0, :], ident[:])
                    t.transpose(ps[:, 4, 2 * P:3 * P], h0[:, 1, :], ident[:]).then_inc(S["ctok_ready"], 1)
                    gemm_half(1, 0)
                    bank5_free(2)
                    rows_of(2)
                    pe.wait_ge(S["ctok_taken"], j0 + i + 1)
                    for n in range(LC - 1):
                        mm = t.matmul(ps[:, 4, n * P:n * P + P], btok[:, n, :], xdw[:, 2, n, :], start=True, stop=True)
                    mm.then_inc(S["hf_ready"], 1)
                    gemm_half(1, 1)
                    section(2)
                    section(3)
                    bank5_free(3)
                    rows_of(3)
                    pe.wait_ge(S["hf_taken"], j0 + i + 1)
                    for n in range(LC - 1):
                        mm = t.matmul(ps[:, 4, n * P:n * P + P], btok[:, n + 1, :], xdw[:, 3, n + 1, :], start=True, stop=True)
                    mm.then_inc(S["hb_ready"], 1)
                    gemm_half(2, 0)
                    bank5_free(4)
                    for h in range(2):
                        for r in range(2):
                            lhs = col[:, LC * KINDS + K_DA, r, h:h + 1].broadcast_to([P, P])
                            mm = t.matmul(ps[:, 5, (2 * h + r) * P:(2 * h + r + 1) * P], lhs, tri[:, r, :], start=True, stop=True)
                    mm.then_inc(S["rows_ready"], 1)
                    gemm_half(2, 1)

                    def outputs(h):
                        pe.wait_ge(S["m_ready"], 3 * (j0 + i) + h + 1)
                        if h == 0:
                            pe.wait_ge(S["hb_taken"], j0 + i + 1)
                        hc = slice(64 * h, 64 * h + 64)
                        for n in range(LC):
                            out, cols = ps[64 * h:64 * h + 64, 6, n * P:n * P + P], slice(n * P, n * P + P)
                            for r in range(2):
                                t.matmul(out, xdw[:, r, n, hc], mbuf[:, 2 * h + r, cols], start=(r == 0), stop=False)
                            for r in range(2):
                                mm = t.matmul(out, hin[:, r, n, hc], cs[:, 2 * h + r, cols], start=False, stop=(r == 1))
                        return mm

                    section(4)
                    section(5)
                    section(6)
                    outputs(0)
                    ada_columns(4, 3 * P)
                    section(7)
                    gemm_half(3, 0)
                    outputs(1).then_inc(S["y_ready"], 1)
                    pe.wait_ge(S["row_copied"], 2 * (j0 + i) + 2)
                    ada_columns(4, 3 * P + 2 * ADA_N // P)
                    pe.wait_ge(S["m_ready"], 3 * (j0 + i) + 3)
                    for r in range(2):
                        t.matmul(ps[:, 4, r * P:r * P + P], xdw[:, 2 + r, LC, :], btok[:, LC, :], start=True, stop=True)
                    for h in range(2):
                        for r in range(2):
                            mm = t.matmul(ps[64 * h:64 * h + 64, 4, 2 * P:3 * P], xdw[:, r, LC, 64 * h:64 * h + 64],
                                          mbuf[:, 4, (2 * h + r) * P:(2 * h + r + 1) * P], start=(r == 0), stop=(r == 1))
                    mm.then_inc(S["cstate_ready"], 1)
                    gemm_half(3, 1)
            norm_stats(1)
            with pe.Fori(0, C // 2) as i:
                adas = 0
                for t_slot, kind in enumerate(OUT_RING):
                    at_ring = t_slot % RING
                    if kind == "a":
                        ada_tile(5, SLOT_OUT, len(OUT_RING), i, t_slot, adas)
                        adas += 1
                        continue
                    n = OUT_RING[:t_slot].count("m")
                    pe.wait_ge(S["low_split"], SLOT_OUT + t_slot + 1 + len(OUT_RING) * i)
                    if n < 2:
                        tile_free(TILE_OUT, 2, i, n)
                        mm = half_slot(n, at_ring, range(C), act_hi, yb_lo, True, False, before=("yb_ready", 1))
                    else:
                        mm = half_slot(n - 2, at_ring, range(C // 2), act_lo, xs_lo, False, False, before=("act_ready", C + 1))
                        if n == 2:
                            pe.wait_ge(S["row_copied"], 2 * C + 1 + i)
                            pe.wait_ge(S["mod_ready"], 1 + C + i)
                            ada_columns(4, 0)
                        mm = half_slot(n - 2, at_ring, range(C // 2, C), act_lo, xs_lo, False, True, before=("act_ready", C + 1))
                    mm.then_inc(S["slot_used"], 1)

            def ffn(lay):
                b, tb, ready = SLOT_FFN[lay], TILE_FFN[lay], lay * FC
                for f0, nf in FPARTS:
                    with pe.Fori(0, nf // 2) as i:
                        for s in range(4):
                            whole_tile(b, i, s, tb, 4, s, norm=(2, 4)[lay] if f0 == 0 else None)
                    b, tb, ready = b + 2 * nf, tb + 2 * nf, ready + nf

                    def down_tile(i, m, between=None):
                        k = m % 2
                        for q in range(2):
                            slot_ready(b, i, 2 * m + q)
                            if q == 0:
                                tile_free(tb, 2, i, m)
                            elif between is not None:
                                between()
                            half_slot(k, (2 * m + q) % RING, range(nf // 2), f_hi, f_lo, q == 0, q == 1, k0=q * (nf // 2),
                                      before=("ffn_ready", ready - nf + q * (nf // 2) + 1) if k == 0 or f0 > 0 and lay == 1 else None
                                      ).then_inc(S["slot_used"], 1)

                    if f0 == 0 or lay == 0:
                        with pe.Fori(0, C // 2) as i:
                            for m in range(2):
                                down_tile(i, m)
                    else:
                        down_tile(0, 0)
                        with pe.Fori(0, C // 2 - 1) as i:
                            for m in (1, 2):
                                down_tile(i, m, between=lambda: turn_out(i, m - 1))
                        down_tile(C // 2 - 1, 1, between=lambda: turn_out(C // 2 - 1, 0))
                        turn_out(C // 2 - 1, 1)
                    b, tb = b + 2 * C, tb + C

            def turn_out(i, k):
                m = 2 * i + k
                pe.wait_ge(S["gx_ready"], m + 1)
                pe.wait_ge(S["out_copied"], m + 1)
                for n in range(LC):
                    t.transpose(ps[:, 4 + k, n * P:n * P + P], gx[:, k, LAT0 + n * P:LAT0 + n * P + P], ident[:])
                t.transpose(ps[:, 6 + k, 0:P], gx[:, k, 0:NCTX], ident[:]).then_inc(S["gx_turned"], 1)

            norm_stats(2)
            ffn(0)
            norm_stats(3)

            def v_windows(i, s):
                pe.wait_ge(S["v_windowed"], 4 * i + s + 1)
                pe.wait_ge(S["v_taken"], 4 * i + s + 1)
                bank = 4 + 2 * (s % 2)
                for w in range(8):
                    mm = t.transpose(ps[:, bank + w // 4, (w % 4) * P:(w % 4) * P + P], vwin[:, w * P:w * P + P], ident[:])
                mm.then_inc(S["v_transposed"], 1)

            with pe.Fori(0, 2) as i:
                for s in range(4):
                    whole_tile(SLOT_QKV, i, s, TILE_QKV, 4, s, norm=3)
                    if s > 0:
                        v_windows(i, s - 1)
                v_windows(i, 3)
            pe.wait_ge(S["caches_loaded"], 32)
            pe.wait_ge(S["v_taken"], 2 + C)
            for n in range(C):
                mm = t.transpose(ps[:, 4 + n // 4, (n % 4) * P:(n % 4) * P + P], kc[:, n * P:n * P + P], ident[:])
            mm.then_inc(S["kc_transposed"], 1)
            for part in (1, 2):
                with pe.Fori(0, 2) as i:
                    for s in range(4):
                        whole_tile(SLOT_QKV + part * C, i, s, TILE_QKV + part * C, 4, s)

            for s in range(2):
                pe.wait_ge(S[f"tile_free{s}"], TILE_NA // 2)
            pe.wait_ge(S["v_taken"], 2 + C)
            def scores(i, u):
                h, b = u // NC, u % NC
                if b == 0:
                    pe.wait_ge(S["q_taken"], 2 * i + h + 1)
                pe.wait_ge(S["scores_taken"], 10 * i + u + 1)
                q = qz[:, h, b * P:b * P + P]
                if b < LC:
                    src = kt[:, bass.ds(i * TQ + WIN[b], NLAT - GRID_W + SPAN)]
                    grid = bass.AP(tensor=src.tensor, offset=src.offset, ap=[src.ap[0], [QW, 2], [GRID_W, ROWS], [1, QW]])
                    t.matmul(ps[:, u % 2, 0:256], q, grid, start=True, stop=True)
                    mm = t.matmul(ps[:, u % 2, 256:384], q, kct[:, bass.ds(i * P, P)], start=True, stop=True)
                else:
                    mm = t.matmul(ps[:, u % 2, 256:384], q, kt[:, bass.ds(i * TQ + NLAT, NCTX)], start=True, stop=True)
                mm.then_inc(S["scores_ready"], 1)

            def turn(i, u):
                pe.wait_ge(S["probs_ready"], 10 * i + u + 3)
                pe.wait_ge(S["pt_copied"], 10 * i + u + 1)
                for k in range(3) if u % NC < LC else [2]:
                    mm = t.transpose(ps[:, 2 + u % 2, k * P:k * P + P], pbf[:, u % 2, k * P:k * P + P], ident[:])
                mm.then_inc(S["pt_ready"], 1)

            def values(i, u):
                h, b = u // NC, u % NC
                pe.wait_ge(S["pt_copied"], 10 * i + u + 3)
                if b == 0:
                    pe.wait_ge(S["o_taken"], 2 * i + h + 1)
                out, cols = ps[:, 4 + h, b * 64:b * 64 + 64], bass.ds(i * P + 64 * h, 64)
                if b < LC:
                    for k in range(2):
                        t.matmul(out, ptb[:, u % 2, k * P:k * P + P], vtok[:, WIN[b] // 8 + 2 * k, cols], start=(k == 0), stop=False)
                    mm = t.matmul(out, ptb[:, u % 2, 256:384], vc[:, cols], start=False, stop=True)
                else:
                    mm = t.matmul(out, ptb[:, u % 2, 256:384], vtok[:, 7, cols], start=True, stop=True)
                mm.then_inc(S["o_ready"], 1)

            def turn_outputs(i):
                pe.wait_ge(S["o_taken"], 2 * i + 4)
                pe.wait_ge(S["o_low"], i + 1)
                for n in range(LC):
                    t.transpose(ps[:, 6, n * P:n * P + P], ot[:, n, :], ident[:])
                t.transpose(ps[:, 7, P:2 * P], kx[:], ident[:])
                t.transpose(ps[:, 7, 0:P], ot[:, LC, :], ident[:]).then_inc(S["o_transposed"], 1)

            def step(i, u, last=None):
                scores(i, u)
                for lag, work in ((2, turn), (3, values)):
                    if u >= lag:
                        work(i, u - lag)
                    elif last is not None:
                        work(last, u - lag + UNITS)

            for u in range(NC):
                step(0, u)
            with pe.Fori(0, C - 1) as i:
                for u in range(NC, UNITS):
                    step(i, u)
                for u in range(NC):
                    step(i + 1, u, i)
                turn_outputs(i)
            for u in range(NC, UNITS):
                step(C - 1, u)
            turn(C - 1, UNITS - 2)
            values(C - 1, UNITS - 3)
            turn(C - 1, UNITS - 1)
            values(C - 1, UNITS - 2)
            values(C - 1, UNITS - 1)
            turn_outputs(C - 1)

            pe.wait_ge(S["o_low"], C + 1)
            for part in range(2):
                for s in range(4):
                    whole_tile(SLOT_NA + 4 * part, 0, s, TILE_NA + 4 * part, 4, s)
            norm_stats(4)
            ffn(1)
            pe.wait_ge(S["squares_used"], 6 * C)
            pe.wait_ge(S["tile_free0"], (TILE_FFN[1] + FFN_TILES) // 2)
            for n in range(NC):
                c0 = LAT0 + n * P if n < LC else 0
                mm = t.matmul(ps[:, 0, 2 * n:2 * n + 2], acc[:, c0:c0 + P], ones[:, 0:2], start=True, stop=True)
            mm.then_inc(S["token_sums"], 1)

        @block.scalar
        def _(act):
            a = nc.scalar.activation
            st = Steps(act, S["act"])

            def split(b, i, s):
                act.wait_ge(S[f"raw_loaded{s % RAW}"], slot16(b, i, s))
                if not (isinstance(i, int) and b + s + 4 * i < RING):
                    act.wait_ge(S["slot_used"], b + s - RING + 1 + 4 * i)
                a(w_hi[:, s], raw[:, s % RAW], ACT.Copy).then_inc(S["high_split"], 1)

            def used(b, i, s):
                act.wait_ge(S["slot_used"], b + s + 1 + 4 * i)

            def square(n, src, c):
                if not (n == 0 and isinstance(c, int) and c == 0):
                    act.wait_ge(S["squares_used"], C * n + c)
                a(sq[:], src[:, bass.ds(c * T, T)], ACT.Square).then_inc(S["squares_ready"], 1)

            def root(n):
                bank = 2 if n == 0 else 6
                a(eps[:, 1:2], eps[:, 0:1], ACT.Sqrt)
                act.wait_ge(S["squares_summed"], n + 1)
                a(F(rms[:]), ps[:, bank:bank + 2, 0:HALF], ACT.Sqrt, scale=1.0 / D, bias=eps[:, 0:1]).then_inc(S["rms_ready"], 1)

            def scaled(n, c):
                act.wait_ge(S["scaled_ready"], C * n + 1 + c)

            def normed(n, c, s, shift):
                scaled(n, c)
                for lo, hi, stream in STREAMS:
                    ins = a(act_hi[:, bass.ds(c * T + lo, hi - lo)], nt[:, s, lo:hi], ACT.Identity,
                            bias=mod[:].rearrange("p m c s -> p (m c s)")[:, bass.ds((shift * C + c) * 2 + stream, 1)])
                ins.then_inc(S["act_high"], 1)

            def norm(n, shift):
                root(n)
                with act.Fori(0, C // 2) as i:
                    for s in range(2):
                        normed(n, 2 * i + s, s, shift)

            def ring_split(slot, base, per, i, t):
                src, loaded, value = slot
                act.wait_ge(loaded, value)
                act.wait_ge(S["slot_used"], base + t - RING + 1 + per * i)
                a(w_hi[:, t % RING], src, ACT.Copy).then_inc(S["high_split"], 1)

            def mix_split(j, t):
                ring_split(mix_slot(j, t), SLOT_MIX, len(MIX_RING), j, t)

            def out_split(i, t):
                ring_split(out_slot(i, t), SLOT_OUT, len(OUT_RING), i, t)

            def copy_row(bank, used_at, squared):
                act.wait_ge(S["slot_used"], used_at)
                act.wait_ge(S["squares_used"], squared)
                a(arow[:], ps[0:4, bank, :], ACT.Copy).then_inc(S["row_copied"], 1)

            act.wait_ge(S["par_ready"], 1)
            a(csth[:].rearrange("p s k -> p (s k)"), par[:, R_C:R_C + 2 * C], ACT.Tanh, scale=0.5).then_inc(S["csil_tanh"], 1)
            act.wait_ge(S["consts_ready"], 2)
            for c0 in range(C):
                act.wait_ge(S["x_copied"], c0 + 1)
                square(0, x, c0)
            for n, bank in enumerate((7, 4, 0, 1)):
                if n == 3:
                    root(0)
                act.wait_ge(S["first_summed"], 2 * n + 2)
                a(frow[:, n * 4 * P:(n + 1) * 4 * P], ps[0:2, bank, :], ACT.Copy).then_inc(S["first_copied"], 1)
            for s in range(RAW):
                split(SLOT_IN, 0, s)
            act.wait_ge(S["wdt_loaded"], 16)
            a(wdt_hi[:], wdt[:], ACT.Copy).then_inc(S["wdt_high"], 1)
            act.wait_ge(S["dskip_loaded"], 48)
            a(dtb[:, 1, :], dtb[:, 1, :], ACT.Exp).then_inc(S["a_exp"], 1)
            with act.Fori(0, C // 2) as i:
                for s in range(2):
                    normed(0, 2 * i + s, s, 0)
            for s in range(RAW, 4):
                split(SLOT_IN, 0, s)
            act.wait_ge(S["csil_ready"], 1)
            a(csil_r[:, :, 0:2], csil[:], ACT.Copy).then_inc(S["csil_high"], 1)

            def conv_in(b, i, s, ci, n):
                used(b, i, s)
                w1, wb = halfw[:, bass.ds(XBC + ci, 1)], halfw[:, bass.ds(3 * XBC + ci, 1)]
                a(F(cgs[:]), V(s % 2), ACT.Identity, scale=w1, bias=wb)
                a(F(gpad[:, 1:T + 1]), V(s % 2), ACT.Copy).then_inc(S[f"tile_free{s % 2}"], 1)
                act.wait_ge(S["conv_ready"], n + 1)
                a(zs[:], cgs[:], ACT.Tanh).then_inc(S["conv_tanh"], 1)
                if b + 4 * i + s + 4 < SLOT_MIX:
                    split(b + 4, i, s)
                else:
                    mix_split(0, s)
                act.wait_ge(S["xin_ready"], n + 1)

            act.wait_ge(S["dt_summed"], 1)
            a(F(dtrow[:]), ps[0:2 * HEADS, 5:7, 0:HALF], ACT.Copy).then_inc(S["dtrow_ready"], 1)
            act.wait_ge(S["dt_exp"], 1)
            a(dtt[:, 1, :], dtt[:, 1, :], ACT.Exp).then_inc(S["dt_exp"], 1)
            for s in range(4):
                conv_in(SLOT_IN, 0, s, C + s, s)
            act.wait_ge(S["sums_ready"], 1)
            act.wait_ge(S["sc_ready"], 2)
            sums_ps = ps[:, 6, 0:NC * 96].rearrange("p (n q) -> p n q", n=NC)
            a(sc[:, :, K_END, :], sums_ps[:, :, 32:64], ACT.Exp)
            a(sc[:, :, K_DEC, :], sums_ps[:, :, 64:96], ACT.Exp).then_inc(S["sums_exp"], 1)
            for i in range(2):
                for s in range(4):
                    conv_in(SLOT_IN + 4, i, s, 4 * i + s, 4 * i + 4 + s)

            for g in range(GROUPS):
                j0 = (C // GROUPS) * g
                with act.Fori(0, C // GROUPS) as i:
                    j = j0 + i
                    MAIN = [t for t, kind in enumerate(MIX_RING) if kind == "m"]

                    def main_used(s):
                        act.wait_ge(S["slot_used"], SLOT_MIX + MAIN[s] + 1 + len(MIX_RING) * j)

                    def splits(*slots):
                        for t in slots:
                            mix_split(j, t)

                    def rows_exp(u):
                        act.wait_ge(S["rows_ready"], 5 * (j0 + i) + u + 1)
                        a(cs[:, u, :], ps[:, 5, :], ACT.Exp).then_inc(S["rows_exp"], 1)

                    def seg_exp(u):
                        act.wait_ge(S["seg_ready"], 5 * (j0 + i) + u + 1)
                        a(mbuf[:, u, :], mbuf[:, u, :], ACT.Exp).then_inc(S["seg_exp"], 1)

                    act.wait_ge(S["prep_ready"], j0 + i + 1)
                    rows_exp(0)
                    seg_exp(0)
                    main_used(0)
                    a(F(zs[:]), V(0), ACT.Tanh, scale=0.5).then_inc(S["gate_tanh"], 1)
                    splits(4)
                    rows_exp(1)
                    seg_exp(1)
                    splits(5, 6)
                    rows_exp(2)
                    seg_exp(2)
                    main_used(1)
                    a(F(cgs[:]), V(1), ACT.Copy).then_inc(S["tile_free1"], 1)
                    splits(7, 8)
                    rows_exp(3)
                    seg_exp(3)
                    copy_row(7, SLOT_MIX + MAIN[2] + len(MIX_RING) * j, C + j)
                    splits(9)
                    seg_exp(4)
                    act.wait_ge(S["tile_free0"], (TILE_MIX + 4 * j0) // 2 + 2 + 2 * i)
                    splits(10)
                    a(cgs[:], gpad[:, 1:T + 1], ACT.Copy, scale=par[:, bass.ds(R_SCW + C + j0 + i, 1)]).then_inc(S["conv_scaled"], 1)
                    splits(11, 12, 13)
                    act.wait_ge(S["mod_turned"], 2 * j + 1)
                    copy_row(7, SLOT_MIX + MAIN[3] + len(MIX_RING) * j, C + j)
                    splits(14)
                    act.wait_ge(S["cstate_taken"], j0 + i + 1)
                    for r in range(2):
                        act.dma_start(new_state[0, 0, r].rearrange("h p n -> (h p) n")[bass.ds((j0 + i) * P, P), :],
                                      sto[:, r, :]).then_inc(S["cstate_stored"], 16)
                    act.wait_ge(S["ya_ready"], j0 + i + 1)
                    square(1, xs, j0 + i)
                    splits(15)
                    act.wait_ge(S["cstate_stored"], 32 * (j0 + i) + 32)

            act.wait_ge(S["slot_used"], SLOT_OUT)
            act.wait_ge(S["tile_free1"], TILE_OUT // 2)
            act.wait_ge(S["mod_ready"], 1 + C)
            act.wait_ge(S["cstate_stored"], 32 * C)
            act.dma_start(x[:], x_dram).then_inc(S["x_reloaded"], 16)
            with act.Fori(0, C) as i:
                a(act_hi[:, bass.ds(i * T, T)], yb[:, bass.ds(i * T, T)], ACT.Copy).then_inc(S["yb_high"], 1)
            root(1)
            between = {1: 4, 2: 5, 4: 6}
            for c0 in range(C):
                scaled(1, c0)
                a(act_lo[:, c0 * T:c0 * T + T], nt[:, c0 % 2], ACT.Copy).then_inc(S["act_high"], 1)
                if c0 in between:
                    out_split(0, between[c0])

            def only_splits(b, count):
                with act.Fori(0, count) as i:
                    for s in range(4):
                        split(b + 4, i, s)

            def tiles_added(n, b, tb, last_slot, splits):
                def turn(i, splits):
                    for s in range(4):
                        if splits:
                            split(b + 4, i, s)
                        if s in last_slot:
                            k = last_slot.index(s)
                            act.wait_ge(S[f"tile_free{k}"], tb // 2 + 1 + i)
                            square(n, x, 2 * i + k)
                            if n == 5:
                                act.wait_ge(S["gx_turned"], 2 * i + k + 1)
                                a(gx[:, k], x[:, bass.ds((2 * i + k) * T, T)], ACT.Copy, scale=par[:, bass.ds(R_FIN + k + 2 * i, 1)]
                                  ).then_inc(S["gx_ready"], 1)

                if n == 5:
                    act.sem_inc(S["gx_turned"], 2)
                    act.sem_inc(S["out_copied"], 2)
                with act.Fori(0, C // 2 - 1) as i:
                    turn(i, True)
                turn(C // 2 - 1, splits)

            def out_turn(i, first=4, last=False):
                def next_splits(*slots):
                    for t in slots:
                        if last and t >= len(OUT_RING):
                            split(SLOT_FFN[0], 0, t - len(OUT_RING))
                        else:
                            out_split(i, t)

                next_splits(*range(first, 8))
                copy_row(5, SLOT_OUT + 6 + len(OUT_RING) * i, 2 * C + 2 * i)
                next_splits(8, 9)
                for k in range(2):
                    next_splits(10 + k)
                    act.wait_ge(S[f"tile_free{k}"], TILE_OUT // 2 + 1 + i)
                    square(2, x, 2 * i + k)

            out_turn(0, first=7)
            with act.Fori(1, C // 2 - 1) as i:
                out_turn(i)
            out_turn(C // 2 - 1, last=True)

            def ffn(lay):
                b, tb = SLOT_FFN[lay], TILE_FFN[lay]
                f = lay * FC
                for f0, nf in FPARTS:
                    with act.Fori(0, nf // 2) as i:
                        for k in range(2):
                            used(b, i, 2 * k)
                            w1 = par[:, bass.ds(R_FW[lay] + FC + f0 + k + 2 * i, 1)]
                            a(F(ft[k][:]), V(0), ACT.Copy, scale=w1)
                            a(F(fg[k][:, 1:T + 1]), V(0), ACT.Copy).then_inc(S["tile_free0"], 1)
                            split(b + 4, i, 2 * k)
                            act.wait_ge(S["ffn_conv"], f + f0 + k + 1 + 2 * i)
                            a(fe[k][:], ft[k][:], ACT.Gelu_apprx_tanh).then_inc(S["ffn_gelu"], 1)
                            act.wait_ge(S["tile_free1"], (tb + 2 * k) // 2 + 1 + 2 * i)
                            a(f_hi[:, bass.ds((2 * i + k) * T, T)], fa[k][:], ACT.Copy).then_inc(S["ffn_high"], 1)
                            split(b + 4, i, 2 * k + 1)
                    b += 2 * nf
                    tb += 2 * nf
                    if f0 == 0:
                        only_splits(b, C // 2)
                    else:
                        tiles_added(3 + 2 * lay, b, tb, [1, 3], b + 2 * C < ALL_SLOTS)
                    b, tb = b + 2 * C, tb + C

            norm(2, 3)
            ffn(0)

            norm(3, MODS)
            act.sem_inc(S["v_taken"], 2)

            def v_taken(i, s):
                act.wait_ge(S["v_transposed"], 4 * i + s + 1)
                for h in range(2):
                    ins = a(vtok[:, 4 * h:4 * h + 4, bass.ds((4 * i + s) * P, P)],
                            ps[:, 4 + 2 * (s % 2) + h, :].rearrange("p (w n) -> p w n", w=4), ACT.Copy)
                ins.then_inc(S["v_taken"], 1)

            with act.Fori(0, 2) as i:
                for s in range(4):
                    split(SLOT_QKV + 4, i, s)
                    v_taken(i, s)
            act.wait_ge(S["kc_transposed"], 1)
            a(kct[:].rearrange("p (b n) -> p b n", b=2), ps[:, 4:6, :], ACT.Copy).then_inc(S["kc_ready"], 1)
            only_splits(SLOT_QKV + C, 2)
            with act.Fori(0, 2) as i:
                for s in range(4):
                    used(SLOT_QKV + 2 * C, i, s)
                    q0 = (4 * i + s) * TQ
                    scale = HD ** -0.5
                    a(qt[:, bass.ds(q0 + NLAT, NCTX)], ps[:, 2 * (s % 2), 0:NCTX], ACT.Copy, scale=scale)
                    a(qt[:, bass.ds(q0, NB0)], ps[:, 2 * (s % 2), LAT0:HALF], ACT.Copy, scale=scale)
                    a(qt[:, bass.ds(q0 + NB0, HALF)], ps[:, 2 * (s % 2) + 1, 0:HALF], ACT.Copy, scale=scale
                      ).then_inc(S[f"tile_free{s % 2}"], 1)
                    split(SLOT_QKV + 2 * C + 4, i, s)

            act.sem_inc(S["probs_ready"], 2)
            act.sem_inc(S["pt_copied"], 2)
            def probs(i, u):
                act.wait_ge(S["scores_taken"], 10 * i + u + 3)
                act.wait_ge(S["pt_ready"], 10 * i + u + 1)
                c0 = 0 if u % NC < LC else 256
                a(pbf[:, u % 2, c0:384], sbf[:, u % 2, c0:384], ACT.Exp, scale=-1.0, bias=nmax[:, u % 2:u % 2 + 1],
                  accum_out=sums[:, u // NC, u % NC:u % NC + 1]).then_inc(S["probs_ready"], 1)

            def pt_copy(i, u):
                act.wait_ge(S["pt_ready"], 10 * i + u + 3)
                act.wait_ge(S["o_ready"], 10 * i + u + 1)
                c0 = 0 if u % NC < LC else 256
                a(ptb[:, u % 2, c0:384], ps[:, 2 + u % 2, c0:384], ACT.Copy).then_inc(S["pt_copied"], 1)

            def outputs_high(i):
                act.wait_ge(S["o_transposed"], i + 1)
                a(act_hi[:, bass.ds(i * T + LAT0, NLAT)].rearrange("p (r b c) -> p b r c", r=ROWS, b=QB),
                  ps[:, 6, :].rearrange("p (b r c) -> p b r c", b=QB, r=ROWS), ACT.Copy)
                a(act_hi[:, bass.ds(i * T, NCTX)], ps[:, 7, 0:NCTX], ACT.Copy).then_inc(S["o_high"], 1)

            def attend(i, u, last=None):
                if u >= 2:
                    pt_copy(i, u - 2)
                elif last is not None:
                    pt_copy(last, u - 2 + UNITS)
                probs(i, u)

            for u in range(NC):
                attend(0, u)
            with act.Fori(0, C - 1) as i:
                for u in range(NC, UNITS):
                    attend(i, u)
                for u in range(NC):
                    attend(i + 1, u, i)
                outputs_high(i)
            for u in range(NC, UNITS):
                attend(C - 1, u)
            for u in (UNITS - 2, UNITS - 1):
                pt_copy(C - 1, u)
            outputs_high(C - 1)
            act.dma_start(new_v[0, 0].rearrange("s h d -> s (h d)"), vtok[:, 7, :]).then_inc(S["k_stored"], 16)
            act.wait_ge(S["o_low"], C + 1)
            act.dma_start(new_k[0, 0].rearrange("s h d -> s (h d)"), kc[:]).then_inc(S["k_stored"], 16)
            act.wait_ge(S["k_stored"], 32)

            for part in range(2):
                for s in range(4):
                    split(SLOT_NA + 4 * part + 4, 0, s)
                    act.wait_ge(S[f"tile_free{s % 2}"], (TILE_NA + 4 * part + s) // 2 + 1)
                    square(4, x, 4 * part + s)
            norm(4, MODS + 3)
            ffn(1)
            a(eps[:, 1:2], eps[:, 0:1], ACT.Sqrt)
            act.wait_ge(S["token_sums"], 1)
            a(root_t[:].rearrange("p n q -> p (n q)"), ps[:, 0, 0:2 * NC], ACT.Sqrt, scale=1.0 / D, bias=eps[:, 0:1]
              ).then_inc(S["token_roots"], 1)
            act.wait_ge(S["token_roots"], 2)
            for n in OUT_ACT:
                a(outs[:, n, :], outs[:, n, :], ACT.Copy, scale=rinv_t[:, n, 0:1]).then_inc(S["act"], 1)
                act.wait_ge(S["act"], OUT_ACT.index(n) + 1)
                act.dma_start(y_sample[0, n * P:n * P + P, :], outs[:, n, :]).then_inc(S["stored"], 16)
            act.wait_ge(S["stored"], 16 * NC)

        @block.vector
        def _(dve):
            v = nc.vector
            st = Steps(dve, S["dve"])
            tt, ts, stt = v.tensor_tensor, v.tensor_scalar, v.scalar_tensor_tensor

            def used(b, i, s):
                dve.wait_ge(S["slot_used"], b + s + 1 + 4 * i)

            def bcast(ap, axis, shape):
                return ap.unsqueeze(axis).broadcast_to(shape)

            dve.wait_ge(S["par_transposed"], 1)
            for n, r in enumerate((112, 120, 3 * FC, 3 * FC)):
                ins = v.tensor_copy(par[:, n * P:n * P + r], ps[:, 4, n * P:n * P + r])
            ins.then_inc(S["par_ready"], 1)
            dve.wait_ge(S["par_ready"], 1)
            st.did(ts(halfw[:], par[:, R_CW:R_CW + 48], 0.5, None, ALU.mult))
            st.did(v.memset(x[:].rearrange("p (c t) -> p c t", c=C)[:, :, NCTX:LAT0], 0.0))
            st.did(v.memset(acc[:], 0.0))
            dve.wait_ge(S["csil_tanh"], 1)
            st.then_wait(stt(csil[:], csth[:].rearrange("p s k -> p k s"), 1.0,
                             par[:, R_C:R_C + 2 * C].rearrange("p (s k) -> p k s", s=2), ALU.add, ALU.mult))
            ts(csil[:], csil[:], 0.5, None, ALU.mult).then_inc(S["csil_ready"], 1)
            tt(sel[:], ident[0:4, 0:2], ident[0:4, 2:4], ALU.add)
            st.wait()

            def add_squares(n, c0):
                dve.wait_ge(S["squares_ready"], C * n + c0 + 1)
                if not (n == 0 and isinstance(c0, int) and c0 == 0):
                    dve.wait_ge(S["squares_used"], C * n + c0)
                tt(acc[:], acc[:], sq[:], ALU.add).then_inc(S["squares_used"], 1)

            for c0 in range(C):
                dve.wait_ge(S["x_transposed"], c0 + 1)
                v.tensor_copy(x[:, c0 * T + LAT0:c0 * T + T], ps[:, 5 + c0 % 2, :])
                v.tensor_copy(x[:, c0 * T:c0 * T + NCTX], ps[:, c0 % 2, 0:NCTX]).then_inc(S["x_copied"], 1)
                if c0 > 0:
                    add_squares(0, c0 - 1)
            add_squares(0, C - 1)
            dve.wait_ge(S["consts_ready"], 2)
            st.then_wait(v.tensor_single_scalar(qi[:, 0:1], qi[:, 0:1], QW - 1, ALU.bitwise_and))
            st.did(v.tensor_copy(qf[:, 0:1], qi[:, 0:1]))
            st.then_wait(v.tensor_copy(qf[:, 4:4 + SPAN], qi[:, 1:1 + SPAN]))
            st.did(ts(qf[:, 1:2], qf[:, 0:1], float(QW // 2), 0.0, ALU.subtract, ALU.max))
            st.did(v.tensor_copy(qf[:, 2:3], qf[:, 0:1]))
            st.then_wait(ts(qf[:, 3:4], qf[:, 0:1], float(QW // 2), None, ALU.min))
            kcf, dist, ok = (qf[:, 4 + n * SPAN:4 + (n + 1) * SPAN] for n in range(3))
            for n, last_col in enumerate((31.0, 31.0, 23.0)):
                st.then_wait(ts(dist, kcf, qf[:, 1 + n:2 + n], -1.0, ALU.add, ALU.mult))
                st.then_wait(ts(dist, dist, last_col, None, ALU.add))
                st.then_wait(ts(ok, dist, 0.0, None, ALU.is_ge))
                st.then_wait(stt(masks[:, n, :], dist, float(QW - 1), ok, ALU.is_le, ALU.mult))
                ins = ts(masks[:, n, :], masks[:, n, :], 1.0, BIG, ALU.subtract, ALU.mult)
                st.did(ins)
            dve.wait_ge(S["first_turned"], C // 2)
            st.then_wait(tt(mod[:, 0:2].rearrange("p m c s -> p (m c) s"), ps[:, 5, 0:4 * C].rearrange("p (m s) -> p m s", s=2),
                            bcast(par[:, R_ADAB:R_ADAB + 2 * C], 2, [P, 2 * C, 2]), ALU.add))
            dve.wait_ge(S["dskip_loaded"], 48)
            for h in range(2):
                hp = slice(64 * h, 64 * h + 64)
                ins = tt(dskip[hp, :], dld[hp, 0, h::2], dld[hp, 1, h::2], ALU.add)
            ins.then_inc(S["mod_ready"], 1)

            def norm_times(src, c0, s, gain):
                if gain is None:
                    for lo, hi, stream in STREAMS:
                        ins = stt(nt[:, s, lo:hi], src[:, bass.ds(c0 * T + lo, hi - lo)],
                                  scale_a[:].rearrange("p c s -> p (c s)")[:, bass.ds(2 * c0 + stream, 1)], rinv[:, lo:hi], ALU.mult, ALU.mult)
                else:
                    ins = stt(nt[:, s], src[:, bass.ds(c0 * T, T)], par[:, bass.ds(gain + c0, 1)], rinv[:], ALU.mult, ALU.mult)
                ins.then_inc(S["scaled_ready"], 1)

            def norm_start(n, sec=None, gain=None):
                if sec is not None:
                    st.did(stt(scale_a[:], mod[:, sec], 1.0, bcast(par[:, gain:gain + C], 2, [P, C, 2]), ALU.add, ALU.mult))
                    for dst in (act_hi, act_lo):
                        st.did(v.tensor_copy(dst[:].rearrange("p (c t) -> p c t", c=C)[:, :, NCTX:LAT0],
                                             zeros[:].rearrange("p (c t) -> p c t", c=C)))
                dve.wait_ge(S["rms_ready"], n + 1)
                st.then_wait(v.reciprocal(rinv[:], rms[:]))

            def new_sum():
                st.then_wait(v.memset(acc[:], 0.0))

            def norm(n, src, dst_hi, dst_lo, shift=None, gain=None):
                def low(c0, s):
                    dve.wait_ge(S["act_high"], C * n + 1 + c0)
                    if shift is None:
                        cols = bass.ds(c0 * T, T)
                        ins = tt(dst_lo[:, cols], nt[:, s], dst_hi[:, cols], ALU.subtract)
                    else:
                        for lo, hi, stream in STREAMS:
                            cols = bass.ds(c0 * T + lo, hi - lo)
                            bias = mod[:].rearrange("p m c s -> p (m c s)")[:, bass.ds((shift * C + c0) * 2 + stream, 1)]
                            ins = stt(dst_lo[:, cols], nt[:, s, lo:hi], bias, dst_hi[:, cols], ALU.add, ALU.subtract)
                    ins.then_inc(S["act_ready"], 1)

                norm_times(src, 0, 0, gain)
                with dve.Fori(0, C // 2 - 1) as i:
                    norm_times(src, 2 * i + 1, 1, gain)
                    low(2 * i, 0)
                    dve.wait_ge(S["act_ready"], C * n + 2 * i + 1)
                    norm_times(src, 2 * i + 2, 0, gain)
                    low(2 * i + 1, 1)
                    dve.wait_ge(S["act_ready"], C * n + 2 * i + 2)
                norm_times(src, C - 1, 1, gain)
                low(C - 2, 0)
                low(C - 1, 1)

            dve.wait_ge(S["wdt_high"], 1)
            tt(wdt_lo[:], wdt[:], wdt_hi[:], ALU.subtract).then_inc(S["wdt_ready"], 1)
            norm_start(0, 1, R_NMIX)
            norm(0, x, act_hi, act_lo, shift=0)
            new_sum()

            dve.wait_ge(S["csil_high"], 1)
            tt(csil_r[:, :, 2:4], csil[:], csil_r[:, :, 0:2], ALU.subtract)
            st.then_wait(v.memset(tab[:], 0.0))
            dve.wait_ge(S["table_loaded"], 16)
            for r in range(DR):
                st.did(v.tensor_copy(tab[:, DR - 1 - r, QW:QW + DC], tabr[:, r, DC - 1::-1]))
            st.wait()
            dve.sem_inc(S["table_ready"], 1)
            xx, ee, zz, qq, pp, mm_ = (dtt[:, n, :] for n in range(6))
            grid = lambda ap: ap.rearrange("p (c n) -> p c n", c=NC)
            dve.wait_ge(S["dt_summed"], 2)
            st.then_wait(tt(grid(xx), ps[:, 5, 0:NC * 32].rearrange("p (c n) -> p c n", c=NC), bcast(dtb[:, 0, :], 1, [P, NC, 32]), ALU.add))
            st.did(ts(mm_, xx, 0.0, None, ALU.max))
            st.then_wait(ts(ee, xx, -1.0, None, ALU.mult))
            tt(ee, ee, xx, ALU.min).then_inc(S["dt_exp"], 1)
            dve.wait_ge(S["dt_exp"], 2)
            st.then_wait(ts(zz, ee, 2.0, None, ALU.add))
            st.then_wait(v.reciprocal(zz, zz))
            st.then_wait(tt(zz, zz, ee, ALU.mult))
            st.then_wait(tt(qq, zz, zz, ALU.mult))
            st.then_wait(ts(pp, qq, 1.0 / 17.0, None, ALU.mult))
            for n in (15, 13, 11, 9, 7, 5, 3):
                st.then_wait(stt(pp, pp, 1.0 / n, qq, ALU.add, ALU.mult))
            st.then_wait(stt(pp, pp, 1.0, zz, ALU.add, ALU.mult))
            st.then_wait(stt(sc[:, :, K_DT, :], grid(pp), 2.0, grid(mm_), ALU.mult, ALU.add))
            dve.wait_ge(S["a_exp"], 1)
            stt(sc[:, :, K_DA, :], sc[:, :, K_DT, :], -1.0, bcast(dtb[:, 1, :], 1, [P, NC, 32]), ALU.mult, ALU.mult
                ).then_inc(S["sc_ready"], 1)
            st.did(v.memset(gpad[:, 0:1], 0.0))
            st.then_wait(v.memset(gpad[:, T + 1:T + 2], 0.0))

            def conv(w, w0, w2, n_cols, buf, dst):
                st.then_wait(stt(dst[:], buf[:, 0:T], w[:, bass.ds(w0, 1)], dst[:], ALU.mult, ALU.add))
                return stt(dst[:], buf[:, 2:T + 2], w[:, bass.ds(w2, 1)], dst[:], ALU.mult, ALU.add)

            def conv_in(tile, i, s, ci, n, dst):
                dve.wait_ge(S[f"tile_free{s % 2}"], tile // 2 + 1 + 2 * i)
                conv(halfw, ci, 2 * XBC + ci, T, gpad, cgs).then_inc(S["conv_ready"], 1)
                dve.wait_ge(S["conv_tanh"], n + 1)
                stt(dst, zs[:], 1.0, cgs[:], ALU.add, ALU.mult).then_inc(S["xin_ready"], 1)

            for s in range(4):
                conv_in(s, 0, s, C + s, s, bc[:, s, :])
            dve.wait_ge(S["sums_ready"], 1)
            sums_ps = ps[:, 6, 0:NC * 96].rearrange("p (n q) -> p n q", n=NC)
            v.tensor_copy(sc[:, :, K_SUM, :], sums_ps[:, :, 0:32]).then_inc(S["sc_ready"], 1)
            dve.wait_ge(S["sums_exp"], 1)
            st.did(tt(sc[:, :, K_END, :], sc[:, :, K_END, :], sc[:, :, K_DT, :], ALU.mult))
            with st.loop(2, 4) as i:
                for s in range(4):
                    conv_in(4 + s, i, s, 4 * i + s, 4 * i + 4 + s, xs[:, bass.ds((4 * i + s) * T, T)])
            dve.wait_ge(S["x_spilled"], 16)
            dve.wait_ge(S["table_stored"], 16)
            dve.wait_ge(S["xin_ready"], IN_SLOTS)

            def modulation(m0, n, cols):
                adab = bcast(par[:, bass.ds(R_ADAB + m0, n)], 2, [P, n, 2])
                tt(mod[:].rearrange("p m c s -> p (m c) s")[:, bass.ds(m0, n), :], cols.rearrange("p (m s) -> p m s", s=2), adab, ALU.add
                   ).then_inc(S["mod_ready"], 1)

            for g in range(GROUPS):
                dve.wait_ge(S["group_summed"], g + 1)
                lat_cols, ctx_cols = slice(0, NLAT), slice(NLAT, NC * P)
                for r in range(2):
                    tt(gm[:, r, lat_cols].rearrange("p (n l) -> p n l", n=LC), ps[:, 5, :].rearrange("p (n l) -> p n l", n=LC),
                       bcast(tri[:, r, :], 1, [P, LC, P]), ALU.mult)
                    tt(gm[:, r, ctx_cols], ps[:, 7, 0:P], tri[:, r, :], ALU.mult)
                v.tensor_copy(btok[:, 0:LC, :], ps[:, 6, :].rearrange("p (n l) -> p n l", n=LC))
                v.tensor_copy(btok[:, LC, :], ps[:, 4, 0:P]).then_inc(S["group_ready"], 1)
                dve.wait_ge(S["group_ready"], g + 1)
                j0 = (C // GROUPS) * g
                tb = TILE_MIX + 4 * j0
                MAIN = [t for t, kind in enumerate(MIX_RING) if kind == "m"]
                with st.loop(C // GROUPS, MIX_STEPS) as i:
                    j = j0 + i
                    st.wait()
                    st.did(v.tensor_copy(xsj[:], xs[:, bass.ds(j * T, T)]))
                    scv = sc[:].rearrange("p n k u -> p (n k u)")[:, bass.ds(2 * j, NC * KINDS * 32 - 14)]
                    pair = bass.AP(tensor=scv.tensor, offset=scv.offset, ap=[scv.ap[0], [32, NC * KINDS], [HEADS, 2], [1, 2]])
                    v.tensor_copy(col[:], pair).then_inc(S["prep_ready"], 1)
                    dve.wait_ge(S["prep_ready"], j + 1)
                    colv = col[:].rearrange("p (n k) r h -> p n k r h", k=KINDS)

                    def weighted(kind, r, q, lo, hi, src):
                        n = hi - lo
                        for h in range(2):
                            hc = slice(64 * h, 64 * h + 64)
                            wt = colv[:, lo:hi, kind, r, h:h + 1].broadcast_to([P, n, 64])
                            ins = tt(xdw[:, q, lo:hi, hc], src[:, :, hc], wt, ALU.mult)
                        return ins

                    def weighted_all(lo, hi, src):
                        for r in range(2):
                            weighted(K_DT, r, r, lo, hi, src)
                            ins = weighted(K_END, r, 2 + r, lo, hi, src)
                        return ins

                    def seg(u):
                        if u < 4:
                            dve.wait_ge(S["rows_exp"], 4 * j + u + 1)
                        else:
                            dve.wait_ge(S["rows_ready"], 5 * j + 5)
                        for n in range(4):
                            total = colv[:, n, K_SUM, u % 2, u // 2:u // 2 + 1] if u < 4 else colv[:, LC, K_SUM, n % 2, n // 2:n // 2 + 1]
                            ins = ts(mbuf[:, u, n * P:n * P + P], ps[:, 5, n * P:n * P + P], total, 0.0, ALU.subtract, ALU.min)
                        ins.then_inc(S["seg_ready"], 1)

                    def decayed(u):
                        dve.wait_ge(S["seg_exp"], 5 * j + u + 1)
                        ins = tt(mbuf[:, u, :], mbuf[:, u, :], gm[:, u % 2, lat_cols], ALU.mult)
                        ins = tt(cs[:, u, :], cs[:, u, :], bc[:, 2 + g, LAT0:T], ALU.mult)
                        return ins

                    def states(r):
                        dve.wait_ge(S["hb_ready" if r else "hf_ready"], j + 1)
                        for q in range(LC - 1):
                            src, dst = (q, q + 1) if r == 0 else (LC - 1 - q, LC - 2 - q)
                            from_ps = q if r == 0 else LC - 2 - q
                            for h in range(2):
                                hc = slice(64 * h, 64 * h + 64)
                                ins = stt(hin[:, r, dst, hc], hin[:, r, src, hc], colv[:, src, K_DEC, r, h:h + 1],
                                          ps[:, 4, from_ps * P + 64 * h:from_ps * P + 64 * h + 64], ALU.mult, ALU.add)
                            if q < LC - 2:
                                st.then_wait(ins)
                        ins.then_inc(S["hb_taken" if r else "hf_taken"], 1)

                    dve.wait_ge(S["xtok_ready"], j + 1)
                    weighted_all(0, LC, ps[:, 4, :].rearrange("p (n q) -> p n q", n=LC)).then_inc(S["xtok_taken"], 1)
                    seg(0)
                    seg(1)
                    dve.wait_ge(S["ctok_ready"], j + 1)
                    weighted_all(LC, NC, ps[:, 4, 0:P].rearrange("p (n q) -> p n q", n=1))
                    v.tensor_copy(hin[:, 0, 0, :], ps[:, 4, P:2 * P])
                    v.tensor_copy(hin[:, 1, LC - 1, :], ps[:, 4, 2 * P:3 * P]).then_inc(S["ctok_taken"], 1)
                    dve.wait_ge(S["ctok_taken"], j + 1)
                    decayed(0)
                    dve.wait_ge(S["gate_tanh"], j + 1)
                    stt(F(zs[:]), F(zs[:]), 1.0, V(0), ALU.add, ALU.mult).then_inc(S["tile_free0"], 1)
                    seg(2)
                    states(0)
                    decayed(1).then_inc(S["m_ready"], 1)
                    seg(3)
                    states(1)
                    decayed(2)
                    seg(4)
                    decayed(3).then_inc(S["m_ready"], 1)
                    dve.wait_ge(S["seg_exp"], 5 * j + 5)
                    m4 = mbuf[:, 4, :].rearrange("p (h q) -> p h q", h=2)
                    for r in range(2):
                        rl = slice(r * P, r * P + P)
                        ins = tt(m4[:, :, rl], m4[:, :, rl], bcast(gm[:, r, ctx_cols], 1, [P, 2, P]), ALU.mult)
                    ins.then_inc(S["m_ready"], 1)
                    dve.wait_ge(S["slot_used"], SLOT_MIX + MAIN[2] + 1 + len(MIX_RING) * j)
                    dve.wait_ge(S["tile_free1"], tb // 2 + 1 + 2 * i)
                    tt(F(gpad[:, 1:T + 1]), V(0), F(cgs[:]), ALU.mult).then_inc(S["tile_free0"], 1)
                    dve.wait_ge(S["conv_scaled"], j + 1)
                    st.then_wait(conv(par, R_SCW + j, R_SCW + 2 * C + j, T, gpad, cgs))
                    dve.wait_ge(S["y_ready"], j + 1)
                    skip = dskip[:, bass.ds(j, 1)]
                    st.then_wait(stt(xsj[:, LAT0:T], xsj[:, LAT0:T], skip, ps[:, 6, :], ALU.mult, ALU.add))
                    st.did(stt(xs[:, bass.ds(j * T + LAT0, NLAT)], xsj[:, LAT0:T], 0.5, zs[:, LAT0:T], ALU.mult, ALU.mult))
                    dve.wait_ge(S["cstate_ready"], j + 1)
                    v.tensor_copy(sto[:].rearrange("p r n -> p (r n)"), ps[:, 4, 0:2 * P]).then_inc(S["cstate_taken"], 1)
                    st.then_wait(stt(xsj[:, 0:NCTX], xsj[:, 0:NCTX], skip, ps[:, 4, 2 * P:3 * P], ALU.mult, ALU.add))
                    st.did(stt(xs[:, bass.ds(j * T, NCTX)], xsj[:, 0:NCTX], 0.5, zs[:, 0:NCTX], ALU.mult, ALU.mult))
                    st.wait()
                    dve.sem_inc(S["ya_ready"], 1)
                    dve.wait_ge(S["slot_used"], SLOT_MIX + MAIN[3] + 1 + len(MIX_RING) * j)
                    tt(F(yb[:, bass.ds(j * T, T)]), V(1), F(cgs[:]), ALU.mult).then_inc(S["tile_free1"], 1)
                    add_squares(1, j)
                    dve.wait_ge(S["mod_turned"], 2 * j + 2)
                    modulation((2 + j) * C, C, ps[:, 4, 3 * P:3 * P + 2 * C])

            with dve.Fori(0, C) as i:
                dve.wait_ge(S["yb_high"], i + 1)
                cols = bass.ds(i * T, T)
                tt(yb_lo[:, cols], yb[:, cols], act_hi[:, cols], ALU.subtract).then_inc(S["yb_ready"], 1)
            norm_start(1)
            norm(1, xs, act_lo, xs_lo, gain=R_SNORM)
            new_sum()

            def residual(slots, k, m, sec, n=None):
                dve.wait_ge(S["slot_used"], slots)
                for bank, lo, hi, col0, stream in PIECES:
                    dst = x[:, bass.ds(m * T + col0, hi - lo)]
                    gate = mod[:].rearrange("p m c s -> p (m c s)")[:, bass.ds(2 * (sec * C + m) + stream, 1)]
                    ins = stt(dst, ps[:, 2 * k + bank, lo:hi], gate, dst, ALU.mult, ALU.add)
                ins.then_inc(S[f"tile_free{k}"], 1)
                if n is not None:
                    add_squares(n, m)

            dve.wait_ge(S["x_reloaded"], 16)
            with dve.Fori(0, C // 2) as i:
                dve.wait_ge(S["mod_turned"], 2 * C + 1 + i)
                modulation((SECS - 2) * C + ADA_N // P * i, ADA_N // P, ps[:, 4, 0:2 * ADA_N // P])
                for k in range(2):
                    residual(SLOT_OUT + 7 + k + len(OUT_RING) * i, k, 2 * i + k, 2, 2)

            def ffn(lay):
                b, tb, f = SLOT_FFN[lay], TILE_FFN[lay], lay * FC
                for k in range(2):
                    st.did(v.memset(fg[k][:, 0:1], 0.0))
                    st.did(v.memset(fg[k][:, T + 1:T + 2], 0.0))
                new_sum()
                for f0, nf in FPARTS:
                    with st.loop(nf // 2, 2) as i:
                        for k in range(2):
                            n = f + f0 + k + 1 + 2 * i
                            dve.wait_ge(S["tile_free0"], (tb + 2 * k) // 2 + 1 + 2 * i)
                            w = R_FW[lay] + f0 + k + 2 * i
                            conv(par, w, w + 2 * FC, T, fg[k], ft[k]).then_inc(S["ffn_conv"], 1)
                            used(b, i, 2 * k + 1)
                            dve.wait_ge(S["ffn_gelu"], n)
                            tt(F(fa[k][:]), V(1), F(fe[k][:]), ALU.mult).then_inc(S["tile_free1"], 1)
                            dve.wait_ge(S["ffn_high"], n)
                            cols = bass.ds((2 * i + k) * T, T)
                            tt(f_lo[:, cols], fa[k][:], f_hi[:, cols], ALU.subtract).then_inc(S["ffn_ready"], 1)
                    b, tb = b + 2 * nf, tb + 2 * nf

                    def down(i, m):
                        residual(b + 2 * m + 2 + 4 * i, m % 2, 2 * i + m, lay * MODS + 5, 3 + 2 * lay if f0 > 0 else None)

                    if f0 == 0 or lay == 0:
                        with dve.Fori(0, C // 2) as i:
                            for m in range(2):
                                down(i, m)
                    else:
                        down(0, 0)
                        with dve.Fori(0, C // 2 - 1) as i:
                            for m in (1, 2):
                                down(i, m)
                                copy_out(i, m - 1)
                        down(C // 2 - 1, 1)
                        for k in range(2):
                            copy_out(C // 2 - 1, k)
                    b, tb = b + 2 * C, tb + C

            def copy_out(i, k):
                m = 2 * i + k
                dve.wait_ge(S["gx_turned"], m + 3)
                v.tensor_copy(outs[:, 0:LC, bass.ds(m * P, P)], ps[:, 4 + k, :].rearrange("p (c n) -> p c n", c=LC))
                v.tensor_copy(outs[:, LC, bass.ds(m * P, P)], ps[:, 6 + k, 0:P]).then_inc(S["out_copied"], 1)

            norm_start(2, 4, R_NFFN)
            norm(2, x, act_hi, act_lo, shift=3)
            ffn(0)

            norm_start(3, MODS + 1, R_NMIX + C)
            norm(3, x, act_hi, act_lo, shift=MODS)

            def reversed_tokens(dst, off, k):
                v.tensor_copy(dst[:, bass.ds(off, HALF)], ps[:, 2 * k + 1, HALF - 1::-1][:, 0:HALF])
                v.tensor_copy(dst[:, bass.ds(off + HALF, NB0)], ps[:, 2 * k, HALF - 1:LAT0 - 1:-1])
                return v.tensor_copy(dst[:, bass.ds(off + NLAT, NCTX)], ps[:, 2 * k, 0:NCTX])

            dve.wait_ge(S["x_spilled"], 32)
            with dve.Fori(0, 2) as i:
                for s in range(4):
                    used(SLOT_QKV, i, s)
                    reversed_tokens(vs, 0, s % 2).then_inc(S[f"tile_free{s % 2}"], 1)
                    dve.wait_ge(S[f"tile_free{s % 2}"], (TILE_QKV + s) // 2 + 1 + 2 * i)
                    dve.wait_ge(S["v_taken"], 4 * i + s + 2)
                    flat = vs[:, 0:NLAT]
                    windows = bass.AP(tensor=flat.tensor, offset=flat.offset, ap=[flat.ap[0], [8, 7], [GRID_W, ROWS], [1, QW]])
                    v.tensor_copy(vwin[:, 0:7 * P].rearrange("p (w r c) -> p w r c", w=7, r=ROWS), windows)
                    v.tensor_copy(vwin[:, 7 * P:8 * P], vs[:, NLAT:TQ]).then_inc(S["v_windowed"], 1)
                    dve.wait_ge(S["v_windowed"], 4 * i + s + 1)
            with dve.Fori(0, 2) as i:
                for s in range(4):
                    used(SLOT_QKV + C, i, s)
                    reversed_tokens(kt, (4 * i + s) * TQ, s % 2).then_inc(S[f"tile_free{s % 2}"], 1)

            dve.wait_ge(S["x_spilled"], 32)
            v.memset(bias[:].rearrange("p h t n -> p (h t) n")[:, :, 256:384], 0.0).then_inc(S["attn_copied"], 1)
            dve.sem_inc(S["bias_used"], 2)
            dve.sem_inc(S["scores_taken"], 2)
            dve.sem_inc(S["pt_ready"], 2)
            dve.sem_inc(S["o_ready"], 2)
            dve.sem_inc(S["o_taken"], 2)
            dve.sem_inc(S["o_low"], 1)
            st.then_wait(v.memset(qz[:], 0.0))
            for s in range(2):
                dve.wait_ge(S[f"tile_free{s}"], TILE_NA // 2)
            dve.wait_ge(S["kc_ready"], 1)
            def queries(i, h):
                hp = slice(64 * h, 64 * h + 64)
                v.tensor_copy(qz[hp, h, 0:NLAT].rearrange("p (b r c) -> p b r c", b=QB, r=ROWS),
                              qt[hp, bass.ds(i * TQ, NLAT)].rearrange("p (r b c) -> p b r c", r=ROWS, b=QB))
                v.tensor_copy(qz[hp, h, NLAT:TQ], qt[hp, bass.ds(i * TQ + NLAT, NCTX)]).then_inc(S["q_taken"], 1)

            def scored(i, u):
                h, blk = u // NC, u % NC
                if blk == 0:
                    dve.wait_ge(S["bias_ready"], 2 * i + h + 1)
                dve.wait_ge(S["scores_ready"], 10 * i + u + 1)
                dve.wait_ge(S["probs_ready"], 10 * i + u + 1)
                v.memset(sums[:, h, blk:blk + 1], 0.0)
                c0 = 0 if blk < LC else 256
                bt = BTYPE[blk] if blk < LC else 0
                v.tensor_tensor_reduce(sbf[:, u % 2, c0:384], ps[:, u % 2, c0:384], bias[:, h, bt, c0:384], -1.0, BIG,
                                       ALU.add, ALU.min, nmax[:, u % 2:u % 2 + 1]).then_inc(S["scores_taken"], 1)
                if blk == NC - 1:
                    dve.wait_ge(S["scores_taken"], 10 * i + u + 3)
                    dve.sem_inc(S["bias_used"], 1)

            def normalized(i, h):
                dve.wait_ge(S["probs_ready"], 10 * i + NC * (h + 1) + 2)
                st.then_wait(v.reciprocal(rsum[:, h, :], sums[:, h, :]))
                dve.wait_ge(S["o_ready"], 10 * i + NC * (h + 1) + 2)
                tt(ot[:, :, 64 * h:64 * h + 64], ps[:, 4 + h, 0:NC * 64].rearrange("p (n d) -> p n d", n=NC),
                   rsum[:, h, :].unsqueeze(2).broadcast_to([P, NC, 64]), ALU.mult).then_inc(S["o_taken"], 1)

            def keys_out(i):
                v.tensor_copy(kx[:], kt[:, bass.ds(i * TQ + NLAT, NCTX)])

            def outputs_low(i):
                dve.wait_ge(S["o_high"], i + 1)
                v.tensor_copy(kc[:, bass.ds(i * P, P)], ps[:, 7, P:2 * P])
                lat = bass.ds(i * T + LAT0, NLAT)
                tt(act_lo[:, lat].rearrange("p (r b c) -> p b r c", r=ROWS, b=QB), ps[:, 6, :].rearrange("p (b r c) -> p b r c", b=QB, r=ROWS),
                   act_hi[:, lat].rearrange("p (r b c) -> p b r c", r=ROWS, b=QB), ALU.subtract)
                cx = bass.ds(i * T, NCTX)
                tt(act_lo[:, cx], ps[:, 7, 0:NCTX], act_hi[:, cx], ALU.subtract).then_inc(S["o_low"], 1)

            def second_head(i, more):
                for u in range(NC, UNITS):
                    scored(i, u)
                    if u == NC and more:
                        queries(i + 1, 0)
                    if u == UNITS - 2:
                        keys_out(i)
                        normalized(i, 0)

            queries(0, 0)
            queries(0, 1)
            for u in range(NC):
                scored(0, u)
            with st.loop(C - 1, 2) as i:
                second_head(i, True)
                queries(i + 1, 1)
                for u in range(NC):
                    scored(i + 1, u)
                    if u == 3:
                        normalized(i, 1)
                outputs_low(i)
            second_head(C - 1, False)
            normalized(C - 1, 1)
            outputs_low(C - 1)
            dve.wait_ge(S["x_reloaded"], 32)
            dve.wait_ge(S["k_stored"], 32)
            new_sum()
            for part in range(2):
                for s in range(4):
                    residual(SLOT_NA + 4 * part + s + 1, s % 2, 4 * part + s, MODS + 2, 4)
            norm_start(4, MODS + 4, R_NFFN + C)
            norm(4, x, act_hi, act_lo, shift=MODS + 3)
            ffn(1)
            dve.wait_ge(S["out_copied"], C + 2)
            dve.wait_ge(S["token_roots"], 1)
            v.reciprocal(rinv_t[:], root_t[:]).then_inc(S["token_roots"], 1)
            dve.wait_ge(S["token_roots"], 2)
            for n in OUT_DVE:
                ts(outs[:, n, :], outs[:, n, :], rinv_t[:, n, 0:1], None, ALU.mult).then_inc(S["out_scaled"], 1)


_INS = ["x_prompt", "x_sample", "state_ssd", "cache_k", "cache_v", "c", "c_ctx", "ada_w", "ada_b", "norm_mix_g", "norm_ffn_g",
        "ssd_w_in", "ssd_conv_w", "ssd_conv_b", "ssd_dt_bias", "ssd_a_log", "ssd_d", "ssd_norm_g", "sc_conv_w", "mix0_w_out",
        "na_w_qkv", "na_rpb", "na_w_out", "ffn_w_gate", "ffn_w_up", "ffn_conv_w", "ffn_w_down", "final_norm_g"]
_OUTS = [(1, NCTX, D), (1, NLAT, D), (1, 1, 2, HEADS, HD, NS), (1, 1, NCTX, HEADS, HD), (1, 1, NCTX, HEADS, HD)]


def kernel(**inputs):
    import numpy as np
    import concourse.bacc as bacc
    from concourse.bass_utils import run_bass_kernel_spmd

    nc = bacc.Bacc("TRN2", target_bir_lowering=False, num_devices=1)
    arrays, args = {}, []
    for name in _INS:
        a = np.ascontiguousarray(inputs[name])
        arrays[f"in_{name}"] = a
        args.append(nc.dram_tensor(f"in_{name}", a.shape, mybir.dt.from_np(a.dtype), kind="ExternalInput").ap())
    for i, shape in enumerate(_OUTS):
        args.append(nc.dram_tensor(f"out_{i}", shape, F32, kind="ExternalOutput").ap())
    trunk(nc, *args)
    r = run_bass_kernel_spmd(nc, [arrays], core_ids=[0])
    return tuple(r.results[0][f"out_{i}"] for i in range(len(_OUTS)))
```
